# Optimizing a Trainium2 kernel written in Bass

```python
import jax, jax.numpy as jnp
from jax import lax
import numpy as np

D_MODEL = 1024
BATCH = 1
SEQ = 1024
DEPTH = 2

N_MIXERS = 4
EPS = 1e-6
D_FF = -(-8 * D_MODEL // (3 * 256)) * 256

GLA_HEADS = 4
GLA_DK = D_MODEL // (2 * GLA_HEADS)
GLA_DV = D_MODEL // GLA_HEADS
GLA_GATE_RANK = 16
GLA_TAU = 16.0
GLA_CHUNK = 64
GLA_IN = 2 * GLA_HEADS * GLA_DK + 2 * GLA_HEADS * GLA_DV + GLA_GATE_RANK

GMLP_D_FFN = 6 * D_MODEL
GMLP_HALF = GMLP_D_FFN // 2
GMLP_GROUPS = 8
GMLP_CHUNK = 128

CONV_WIDTH = 31

NSA_HEADS = 16
NSA_KV_HEADS = 4
NSA_HEAD_DIM = D_MODEL // NSA_HEADS
NSA_CMP_BLOCK = 32
NSA_CMP_STRIDE = 16
NSA_CMP_HIDDEN = 256
NSA_SEL_BLOCK = 64
NSA_TOP_N = 16
NSA_WINDOW = 512
NSA_Q_BLOCK = 128
NSA_IN = NSA_HEADS * NSA_HEAD_DIM + 6 * NSA_KV_HEADS * NSA_HEAD_DIM + 3 * NSA_HEADS

kernel_name = 'hybrid_gla_gmlp_conformer_nsa_trunk'

def n_layers_of(m):
    return len(range(m, DEPTH, N_MIXERS))

def rms_norm(x, g):
    xf = x.astype(jnp.float32)
    y = xf * lax.rsqrt(jnp.mean(xf * xf, axis=-1, keepdims=True) + EPS)
    return y.astype(x.dtype) * g

def layer_norm(x, g, b):
    xf = x.astype(jnp.float32)
    mu = jnp.mean(xf, axis=-1, keepdims=True)
    var = jnp.mean(jnp.square(xf - mu), axis=-1, keepdims=True)
    return ((xf - mu) * lax.rsqrt(var + EPS)).astype(x.dtype) * g + b

def masked_softmax(s, mask):
    s = jnp.where(mask, s.astype(jnp.float32), -1e30)
    return jnp.where(mask, jax.nn.softmax(s, axis=-1), 0.0)

def alibi_slopes(n):
    return 2.0 ** (-8.0 * jnp.arange(1, n + 1, dtype=jnp.float32) / n)

def swiglu(h, w_gate, w_up, w_down):
    return (jax.nn.silu(h @ w_gate) * (h @ w_up)) @ w_down

def gla_mixer(h, w_in, w_gate2, b_gate, g_norm, w_out):
    B, S, _ = h.shape
    H, dk, dv, C = GLA_HEADS, GLA_DK, GLA_DV, GLA_CHUNK
    proj = h @ w_in
    o1, o2, o3, o4 = H * dk, 2 * H * dk, 2 * H * dk + H * dv, 2 * H * dk + 2 * H * dv
    q = proj[..., :o1] * dk ** -0.5
    k = proj[..., o1:o2]
    v = proj[..., o2:o3]
    g_out = proj[..., o3:o4]
    a_lr = proj[..., o4:]
    log_a = jax.nn.log_sigmoid((a_lr @ w_gate2 + b_gate).astype(jnp.float32)) / GLA_TAU

    def to_chunks(t, d):
        return t.reshape(B, S // C, C, H, d).transpose(1, 0, 3, 2, 4)

    qs, ks, vs, ls = to_chunks(q, dk), to_chunks(k, dk), to_chunks(v, dv), to_chunks(log_a, dk)
    causal = jnp.tril(jnp.ones((C, C), dtype=bool))

    def step(state, inp):
        qc, kc, vc, lc = inp
        bcum = jnp.cumsum(lc, axis=2)
        o_inter = jnp.einsum('bhcd,bhde->bhce', qc * jnp.exp(bcum), state)
        diff = bcum[:, :, :, None, :] - bcum[:, :, None, :, :]
        decay = jnp.exp(jnp.where(causal[:, :, None], diff, -jnp.inf))
        attn = jnp.einsum('bhtd,bhsd,bhtsd->bhts', qc, kc, decay)
        o = o_inter + jnp.einsum('bhts,bhse->bhte', attn, vc)
        blast = bcum[:, :, -1:, :]
        k_dec = kc * jnp.exp(blast - bcum)
        state = jnp.exp(blast[:, :, 0, :])[..., None] * state + jnp.einsum('bhcd,bhce->bhde', k_dec, vc)
        return state, o

    state0 = jnp.zeros((B, H, dk, dv), jnp.float32)
    _, o = lax.scan(step, state0, (qs, ks, vs, ls))
    o = o.transpose(1, 0, 3, 2, 4).reshape(B, S, H, dv).astype(h.dtype)
    o = rms_norm(o, g_norm) * jax.nn.silu(g_out.reshape(B, S, H, dv))
    return o.reshape(B, S, H * dv) @ w_out

def gmlp_mixer(h, w_in, b_in, ln_g, ln_b, w_s, b_s, w_out):
    B, S, _ = h.shape
    G, C, E = GMLP_GROUPS, GMLP_CHUNK, GMLP_HALF
    z = jax.nn.gelu(h @ w_in + b_in)
    u, v = z[..., :E], z[..., E:]
    v = layer_norm(v, ln_g, ln_b)
    vc = v.reshape(B, S // C, C, G, E // G)
    ws = w_s * jnp.tril(jnp.ones((C, C), dtype=w_s.dtype))
    sv = jnp.einsum('gts,bnsgc->bntgc', ws, vc) + b_s.T[None, None, :, :, None]
    return (u * sv.reshape(B, S, E)) @ w_out

def conv_mixer(h, w_pw1, b_pw1, w_dw, b_dw, ln_g, ln_b, w_pw2, b_pw2):
    D = h.shape[-1]
    ag = h @ w_pw1 + b_pw1
    y = ag[..., :D] * jax.nn.sigmoid(ag[..., D:])
    y = lax.conv_general_dilated(
        y, w_dw[:, None, :], window_strides=(1,), padding=[(CONV_WIDTH - 1, 0)],
        dimension_numbers=('NWC', 'WIO', 'NWC'), feature_group_count=D) + b_dw
    y = jax.nn.silu(layer_norm(y, ln_g, ln_b))
    return y @ w_pw2 + b_pw2

def nsa_mixer(h, w_in, pe_k, w_ck1, w_ck2, pe_v, w_cv1, w_cv2, w_out):
    B, S, _ = h.shape
    H, G, dh = NSA_HEADS, NSA_KV_HEADS, NSA_HEAD_DIM
    R = H // G
    QB, W, SEL, STR = NSA_Q_BLOCK, NSA_WINDOW, NSA_SEL_BLOCK, NSA_CMP_STRIDE
    Nc = S // STR - 1
    Ns = S // SEL
    top_n = min(NSA_TOP_N, Ns)

    proj = h @ w_in
    q = (proj[..., :H * dh] * dh ** -0.5).reshape(B, S, G, R, dh).transpose(0, 2, 3, 1, 4)
    kv = proj[..., H * dh:H * dh + 6 * G * dh].reshape(B, S, 6, G, dh).transpose(2, 0, 3, 1, 4)
    gates = jax.nn.sigmoid(proj[..., H * dh + 6 * G * dh:].astype(jnp.float32))
    gates = gates.reshape(B, S, G, R, 3).transpose(0, 2, 3, 1, 4)

    def compress(t, pe, w1, w2):
        tc = t.reshape(B, G, S // STR, STR, dh)
        blocks = jnp.concatenate([tc[:, :, :-1], tc[:, :, 1:]], axis=3) + pe
        return jax.nn.gelu(blocks.reshape(B, G, Nc, NSA_CMP_BLOCK * dh) @ w1) @ w2

    k_cmp = compress(kv[0], pe_k, w_ck1, w_ck2)
    v_cmp = compress(kv[1], pe_v, w_cv1, w_cv2)
    k_sel_blocks = kv[2].reshape(B, G, Ns, SEL, dh)
    v_sel_blocks = kv[3].reshape(B, G, Ns, SEL, dh)
    k_win = jnp.pad(kv[4], ((0, 0), (0, 0), (W, 0), (0, 0)))
    v_win = jnp.pad(kv[5], ((0, 0), (0, 0), (W, 0), (0, 0)))

    sl = alibi_slopes(H).reshape(G, R)[None, :, :, None, None]
    c_start = STR * jnp.arange(Nc, dtype=jnp.int32)
    c_last = c_start + NSA_CMP_BLOCK - 1
    c_center = c_start.astype(jnp.float32) + (NSA_CMP_BLOCK - 1) / 2.0
    s_start = SEL * jnp.arange(Ns, dtype=jnp.int32)
    overlap = jnp.clip(jnp.minimum(c_start[:, None] + NSA_CMP_BLOCK, s_start[None] + SEL)
                       - jnp.maximum(c_start[:, None], s_start[None]), 0, None).astype(jnp.float32) / NSA_CMP_BLOCK
    blk = jnp.arange(Ns, dtype=jnp.int32)
    gather = jax.vmap(jax.vmap(lambda kb, ix: kb[ix]))

    def q_block(n):
        q0 = n * QB
        qb = lax.dynamic_slice_in_dim(q, q0, QB, axis=3)
        gb = lax.dynamic_slice_in_dim(gates, q0, QB, axis=3)
        t = q0 + jnp.arange(QB, dtype=jnp.int32)
        tf = t.astype(jnp.float32)
        s_c = jnp.einsum('bgrtd,bgnd->bgrtn', qb, k_cmp).astype(jnp.float32)
        s_c = s_c - sl * (tf[:, None] - c_center[None, :])
        p_c = masked_softmax(s_c, c_last[None, :] <= t[:, None])
        o_c = jnp.einsum('bgrtn,bgnd->bgrtd', p_c, v_cmp)
        imp = jnp.einsum('bgrtn,nj->bgtj', p_c, overlap)
        cur = t // SEL
        forced = (blk[None] == 0) | (blk[None] == cur[:, None]) | (blk[None] == cur[:, None] - 1)
        imp = jnp.where(forced, jnp.inf, jnp.where(blk[None] * SEL <= t[:, None], imp, -jnp.inf))
        _, idx = lax.top_k(imp, top_n)
        k_sel = gather(k_sel_blocks, idx).reshape(B, G, QB, top_n * SEL, dh)
        v_sel = gather(v_sel_blocks, idx).reshape(B, G, QB, top_n * SEL, dh)
        pos = (idx[..., None] * SEL + jnp.arange(SEL, dtype=jnp.int32)).reshape(B, G, QB, top_n * SEL)
        dist_s = t[None, None, :, None] - pos
        s_s = jnp.einsum('bgrtd,bgtkd->bgrtk', qb, k_sel).astype(jnp.float32)
        s_s = s_s - sl * dist_s[:, :, None].astype(jnp.float32)
        p_s = masked_softmax(s_s, (dist_s >= 0)[:, :, None])
        o_s = jnp.einsum('bgrtk,bgtkd->bgrtd', p_s, v_sel)
        kw = lax.dynamic_slice_in_dim(k_win, q0, W + QB, axis=2)
        vw = lax.dynamic_slice_in_dim(v_win, q0, W + QB, axis=2)
        s_pos = q0 - W + jnp.arange(W + QB, dtype=jnp.int32)
        dist_w = t[:, None] - s_pos[None]
        valid_w = (dist_w >= 0) & (dist_w < W) & (s_pos[None] >= 0)
        s_w = jnp.einsum('bgrtd,bgsd->bgrts', qb, kw).astype(jnp.float32)
        s_w = s_w - sl * dist_w.astype(jnp.float32)
        p_w = masked_softmax(s_w, valid_w)
        o_w = jnp.einsum('bgrts,bgsd->bgrtd', p_w, vw)
        return gb[..., 0:1] * o_c + gb[..., 1:2] * o_s + gb[..., 2:3] * o_w

    outs = lax.map(q_block, jnp.arange(S // QB, dtype=jnp.int32))
    o = outs.transpose(1, 0, 4, 2, 3, 5).reshape(B, S, H * dh).astype(h.dtype)
    return o @ w_out

def setup_inputs(seed: int = 0) -> dict:
    key = jax.random.key(seed)
    keys = iter(jax.random.split(key, 64))
    D = D_MODEL
    out_scale = (2.0 * DEPTH) ** -0.5

    def w(shape, fan_in, scale=1.0):
        return jax.random.normal(next(keys), shape, jnp.float32) * (scale * fan_in ** -0.5)

    def gain(shape):
        return 1.0 + 0.05 * jax.random.normal(next(keys), shape, jnp.float32)

    def bias(shape, s=0.02):
        return s * jax.random.normal(next(keys), shape, jnp.float32)

    nA, nB, nC, nD = n_layers_of(0), n_layers_of(1), n_layers_of(2), n_layers_of(3)
    dh = NSA_HEAD_DIM
    return {
        'x': jax.random.normal(next(keys), (BATCH, SEQ, D), jnp.float32),
        'norm_mix': gain((DEPTH, D)),
        'norm_ffn': gain((DEPTH, D)),
        'norm_final': gain((D,)),
        'w_ffn_gate': w((DEPTH, D, D_FF), D),
        'w_ffn_up': w((DEPTH, D, D_FF), D),
        'w_ffn_down': w((DEPTH, D_FF, D), D_FF, out_scale),
        'a_w_in': w((nA, D, GLA_IN), D),
        'a_w_gate2': w((nA, GLA_GATE_RANK, GLA_HEADS * GLA_DK), GLA_GATE_RANK),
        'a_b_gate': bias((nA, GLA_HEADS * GLA_DK), 0.5),
        'a_g_norm': gain((nA, GLA_DV)),
        'a_w_out': w((nA, GLA_HEADS * GLA_DV, D), GLA_HEADS * GLA_DV, out_scale),
        'b_w_in': w((nB, D, GMLP_D_FFN), D),
        'b_b_in': bias((nB, GMLP_D_FFN)),
        'b_ln_g': gain((nB, GMLP_HALF)),
        'b_ln_b': bias((nB, GMLP_HALF)),
        'b_w_s': w((nB, GMLP_GROUPS, GMLP_CHUNK, GMLP_CHUNK), GMLP_CHUNK, 0.5),
        'b_b_s': gain((nB, GMLP_GROUPS, GMLP_CHUNK)),
        'b_w_out': w((nB, GMLP_HALF, D), GMLP_HALF, out_scale),
        'c_w_pw1': w((nC, D, 2 * D), D),
        'c_b_pw1': bias((nC, 2 * D)),
        'c_w_dw': w((nC, CONV_WIDTH, D), CONV_WIDTH),
        'c_b_dw': bias((nC, D)),
        'c_ln_g': gain((nC, D)),
        'c_ln_b': bias((nC, D)),
        'c_w_pw2': w((nC, D, D), D, out_scale),
        'c_b_pw2': bias((nC, D)),
        'd_w_in': w((nD, D, NSA_IN), D),
        'd_pe_k': bias((nD, NSA_CMP_BLOCK, dh)),
        'd_w_ck1': w((nD, NSA_CMP_BLOCK * dh, NSA_CMP_HIDDEN), NSA_CMP_BLOCK * dh),
        'd_w_ck2': w((nD, NSA_CMP_HIDDEN, dh), NSA_CMP_HIDDEN),
        'd_pe_v': bias((nD, NSA_CMP_BLOCK, dh)),
        'd_w_cv1': w((nD, NSA_CMP_BLOCK * dh, NSA_CMP_HIDDEN), NSA_CMP_BLOCK * dh),
        'd_w_cv2': w((nD, NSA_CMP_HIDDEN, dh), NSA_CMP_HIDDEN),
        'd_w_out': w((nD, NSA_HEADS * dh, D), NSA_HEADS * dh, out_scale),
    }

def reference(x, norm_mix, norm_ffn, norm_final, w_ffn_gate, w_ffn_up, w_ffn_down,
              a_w_in, a_w_gate2, a_b_gate, a_g_norm, a_w_out,
              b_w_in, b_b_in, b_ln_g, b_ln_b, b_w_s, b_b_s, b_w_out,
              c_w_pw1, c_b_pw1, c_w_dw, c_b_dw, c_ln_g, c_ln_b, c_w_pw2, c_b_pw2,
              d_w_in, d_pe_k, d_w_ck1, d_w_ck2, d_pe_v, d_w_cv1, d_w_cv2, d_w_out):
    h = x
    for i in range(DEPTH):
        m, j = i % N_MIXERS, i // N_MIXERS
        y = rms_norm(h, norm_mix[i])
        if m == 0:
            y = gla_mixer(y, a_w_in[j], a_w_gate2[j], a_b_gate[j], a_g_norm[j], a_w_out[j])
        elif m == 1:
            y = gmlp_mixer(y, b_w_in[j], b_b_in[j], b_ln_g[j], b_ln_b[j], b_w_s[j], b_b_s[j], b_w_out[j])
        elif m == 2:
            y = conv_mixer(y, c_w_pw1[j], c_b_pw1[j], c_w_dw[j], c_b_dw[j], c_ln_g[j], c_ln_b[j],
                           c_w_pw2[j], c_b_pw2[j])
        else:
            y = nsa_mixer(y, d_w_in[j], d_pe_k[j], d_w_ck1[j], d_w_ck2[j], d_pe_v[j], d_w_cv1[j],
                          d_w_cv2[j], d_w_out[j])
        h = h + y
        h = h + swiglu(rms_norm(h, norm_ffn[i]), w_ffn_gate[i], w_ffn_up[i], w_ffn_down[i])
    return rms_norm(h, norm_final)


_drawn_inputs = setup_inputs


def setup_inputs(seed=0):
    import zlib

    import numpy as np

    out = dict(_drawn_inputs(seed))
    spreads = {}
    factors = {'a_g_norm': 3.522,
     'b_b_in': 8.0,
     'b_ln_g': 21.692,
     'b_ln_b': 54.854,
     'b_b_s': 12.541,
     'norm_ffn': 2.877}
    for name, (base, spread) in spreads.items():
        noise = np.random.default_rng([zlib.crc32(name.encode()), seed]).standard_normal(out[name].shape)
        drawn = base * np.exp(spread * noise) if base else spread * noise
        out[name] = __import__('jax').numpy.asarray(drawn.astype(out[name].dtype))
    for name, factor in factors.items():
        out[name] = (out[name] * factor).astype(out[name].dtype)
    return out
```

```python
from contextlib import ExitStack

import numpy as np

import concourse.bass as bass
from concourse import mybir

F32 = mybir.dt.float32
FR = mybir.dt.float32r
U8 = mybir.dt.uint8
ALU = mybir.AluOpType
ACT = mybir.ActivationFunctionType

P = 128
EPS = 1e-6
BANK = 512
GLA_HEADS = 4
GLA_TAU = 16.0
STAGES = 4
LEVELS = [64, 32, 16, 8, 4, 2, 1]


class WeightBlocks:

    def __init__(self, phases):
        self.phase, self.slot, self.landed, self.before = {}, [], [], []
        value, last = [0] * STAGES, [0] * STAGES
        for name, iterations, dmas, slots in phases:
            self.phase[name] = (len(self.slot), len(dmas))
            for _ in range(iterations):
                for n_dmas, s in zip(dmas, slots):
                    self.before.append(last[s])
                    value[s] += 16 * n_dmas
                    self.slot.append(s)
                    self.landed.append(value[s])
                    last[s] = len(self.slot)

    def at(self, name, i, b):
        first, per = self.phase[name]
        if isinstance(i, int):
            n = first + per * i + b
            return self.slot[n], self.landed[n], n + 1, self.before[n]
        n = first + per + b
        step = self.landed[n + per] - self.landed[n]
        return (self.slot[n], (i - 1) * step + self.landed[n], (i - 1) * per + (n + 1),
                (i - 1) * per + self.before[n])


def trunk_kernel(nc, x, norm_mix, norm_ffn, norm_final, w_ffn_gate, w_ffn_up, w_ffn_down,
                 a_w_in, a_w_gate2, a_b_gate, a_g_norm, a_w_out,
                 b_w_in, b_b_in, b_ln_g, b_ln_b, b_w_s, b_b_s, b_w_out,
                 level_masks, causal_matrix, identity, out):
    _, S, D = x.shape
    F = w_ffn_gate.shape[2]
    KT = D // P
    TT = S // P
    HALVES = S // BANK
    H = GLA_HEADS
    DK, DV = D // (2 * H), D // H
    RANK = a_w_gate2.shape[1]
    o_k, o_v, o_g, o_a = H * DK, 2 * H * DK, 2 * H * DK + H * DV, 2 * H * DK + 2 * H * DV
    CH = P
    E = b_w_out.shape[1]
    G = b_w_s.shape[1]
    GC = E // G
    GE = GC // P
    FC = 256
    FT = FC // P
    FSTEPS = F // FC
    assert (KT, TT, HALVES, GE, FT) == (8, 8, 2, 3, 2) and F % FC == 0 and DK == P

    x_d = x.rearrange("b (t p) d -> (b t) p d", p=P)
    out_d = out.rearrange("b (t p) d -> (b t) p d", p=P)

    qk_d = nc.dram_tensor("qk_scratch", (2 * H, P, S), F32).ap()
    v_d = nc.dram_tensor("v_scratch", (S, D), F32).ap()
    al_d = nc.dram_tensor("a_lr_scratch", (RANK, S), F32).ap()
    u_d = nc.dram_tensor("gmlp_v_scratch", (G, TT, P, GC), F32).ap()

    ring4 = [b % STAGES for b in range(12)]
    blocks = WeightBlocks([
        ("gla", 1, [1] * 64, ring4[:8] * 8),
        ("ffn0", FSTEPS, [2] * 8 + [1] * 4, ring4),
        ("gv", G // 2, [1] * 16, ring4[:8] * 2),
        ("gp", G, [1] * 14, ring4 + [0, 1]),
        ("ffn1", FSTEPS, [2] * 8 + [1] * 4, ring4)])

    with ExitStack() as top:
        def make(stack, name, shape, dt=F32):
            return stack.enter_context(nc.sbuf_tensor(name, shape, dt))

        def sb(name, shape, dt=F32):
            return make(top, name, shape, dt)

        def sem(name):
            return top.enter_context(nc.semaphore(name))

        ps = top.enter_context(nc.psum_tensor("ps", [P, 8, BANK], F32))

        RING = 6144
        w_hi_main = sb("w_hi_main", [P, RING], FR)
        w_lo_main = sb("w_lo_main", [P, RING], FR)
        stage = sb("stage", [P, STAGES, BANK])
        x_hi = sb("x_hi", [P, KT, S], FR)
        x_lo = sb("x_lo", [P, KT, S], FR)
        ident = sb("ident", [P, P])
        gain_bc = sb("gain_bc", [P, D])
        eps_col = sb("eps_col", [P, 1])
        tick = sb("tick", [P, 1])
        causal = sb("causal", [P, P])
        stats = sb("stats", [P, 5, 3, TT])

        gla = ExitStack()

        def ga(name, shape, dt=F32):
            return make(gla, name, shape, dt)

        early = ExitStack()
        x_in = make(early, "x_in", [P, 2, D])
        xn0 = make(early, "xn0", [P, 2, D])
        evac = make(early, "evac", [P, 4, BANK])
        mask_stage = make(early, "mask_stage", [P, len(LEVELS) + 1, CH])
        al_sb = make(early, "al_sb", [RANK, S])
        wa_stage = make(early, "wa_stage", [P, KT, RANK])
        wa_hi = make(early, "wa_hi", [P, KT, RANK], FR)
        wa_lo = make(early, "wa_lo", [P, KT, RANK], FR)
        early.close()
        xc_hi = ga("xc_hi", [P, KT, CH], FR)
        xc_lo = ga("xc_lo", [P, KT, CH], FR)
        qk = ga("qk", [P, 2 * H, CH])
        al_c = ga("al_c", [RANK, CH])
        log_a = ga("log_a", [P, H * DK])
        bcum = ga("bcum", [P, H * CH])
        ebuf = ga("ebuf", [P, 2, H * CH])
        zbuf = ga("zbuf", [P, 2, H * CH])
        att = ga("att", [P, H, CH])
        q_dec = ga("q_dec", [P, H, CH])
        k_dec = ga("k_dec", [P, H, CH])
        k_dec_t = ga("k_dec_t", [P, H, CH])
        soft = ga("soft", [P, H * DK])
        v_sb = ga("v_sb", [P, D])
        state = ga("state", [P, H, DV])
        y_hi = ga("y_hi", [P, KT, CH], FR)
        y_lo = ga("y_lo", [P, KT, CH], FR)
        g_sb = ga("g_sb", [P, D])
        masks = ga("masks", [P, len(LEVELS) + 1, CH], U8)
        gnorm_bc = ga("gnorm_bc", [P, DV])
        w_gate2 = ga("w_gate2", [RANK, H * DK])
        b_gate = ga("b_gate", [1, H * DK])
        ones = ga("ones", [1, P])
        eb_last = ga("eb_last", [P, H])
        ostat = ga("ostat", [P, 3, H])
        w_hi_more = ga("w_hi_more", [P, 8 * 2 * BANK - RING], FR)
        w_lo_more = ga("w_lo_more", [P, 8 * 2 * BANK - RING], FR)
        gla.close()

        resid = sb("resid", [P, TT, D])
        work = sb("work", [P, 2, D])
        ffn = ExitStack()
        h_hi = make(ffn, "h_hi", [P, FT, S], FR)
        h_lo = make(ffn, "h_lo", [P, FT, S], FR)
        prod = make(ffn, "prod", [P, 2, BANK])
        ffn.close()
        m_hi = sb("m_hi", [P, GE, S], FR)
        m_lo = sb("m_lo", [P, GE, S], FR)
        vn = sb("vn", [P, TT, GC])
        ln_g_bc = sb("ln_g_bc", [P, GC])
        ln_b_bc = sb("ln_b_bc", [P, GC])
        bs_bc = sb("bs_bc", [P, P])
        b_u = sb("b_u", [P, GE])
        ws_raw = sb("ws_raw", [P, P])
        ws_t = sb("ws_t", [P, P])
        st6 = sb("st6", [P, TT, 6])
        st_all = sb("st_all", [P, TT, G, 6])
        mv = sb("mv", [P, TT, 2])
        dev = sb("dev", [P, TT])

        staged = [sem(f"staged_{s}") for s in range(STAGES)]
        w_hi_done, w_lo_done = sem("w_hi_done"), sem("w_lo_done")
        const_ld, wa_ld, wa_hi_done, wa_lo_done, consts_set = (
            sem(n) for n in ("const_ld", "wa_ld", "wa_hi_done", "wa_lo_done", "consts_set"))
        gain_ld, masks_made = sem("gain_ld"), sem("masks_made")
        x_ld = [sem(f"x_ld_{s}") for s in range(2)]
        squared, rooted, inverted, normed, turned, x_hi_done, x_lo_done = (
            [sem(f"{n}_{i}") for i in range(5)]
            for n in ("squared", "rooted", "inverted", "normed", "turned", "x_hi_done", "x_lo_done"))
        al_ready, al_copied, al_stored = sem("al_ready"), sem("al_copied"), sem("al_stored")
        proj_ready, qk_copied, v_copied = sem("proj_ready"), sem("qk_copied"), sem("v_copied")
        evac_stored = [sem(f"evac_stored_{s}") for s in range(4)]
        al_ld, xc_ld, qk_ld, v_ld, y_moved = (sem(n) for n in ("al_ld", "xc_ld", "qk_ld", "v_ld", "y_moved"))
        z_ready, g_ready, cum_ready, y_turned, level_ready, k_turned, o_ready, s_ready = (
            sem(n) for n in ("z_ready", "g_ready", "cum_ready", "y_turned", "level_ready", "k_turned",
                             "o_ready", "s_ready"))
        z_abs, z_exp, z_soft, bcum_done, exp_done, q_exp, k_exp, last_exp, g_silu, k_dec_t_done, o_sq, o_root, \
            y_hi_done = (sem(n) for n in (
                "z_abs", "z_exp", "z_soft", "bcum_done", "exp_done", "q_exp", "k_exp", "last_exp", "g_silu",
                "k_dec_t_done", "o_sq", "o_root", "y_hi_done"))
        q_scaled, log_a_done, z_done, level_kept, qk_decayed, state_done, o_inv, y_done, y_lo_done = (
            sem(n) for n in ("q_scaled", "log_a_done", "z_done", "level_kept", "qk_decayed", "state_done",
                             "o_inv", "y_done", "y_lo_done"))
        exponent_done, g_gained = sem("exponent_done"), sem("g_gained")
        xr_ld = [sem(f"xr_ld_{s}") for s in range(2)]
        ao_ready, ao_added = sem("ao_ready"), sem("ao_added")
        f_names = ("gate_ready", "up_ready", "down_ready", "silu_done", "h_hi_done", "prod_done", "h_lo_done",
                   "down_added")
        fsem = [{n: sem(f"{n}_{layer}") for n in f_names} for layer in range(2)]
        bias_ld = [sem(f"bias_ld_{s}") for s in range(2)]
        gv_ready, gv_biased, gv_gelu, gv_stat, gv_kept, mv_done, dev_done, inv_done = (
            sem(n) for n in ("gv_ready", "gv_biased", "gv_gelu", "gv_stat", "gv_kept", "mv_done", "dev_done",
                             "inv_done"))
        gv_stored = [sem(f"gv_stored_{s}") for s in range(4)]
        ws_ld, bu_ld, ln_ld, vn_ld = (sem(n) for n in ("ws_ld", "bu_ld", "ln_ld", "vn_ld"))
        ws_turned, ws_masked = sem("ws_turned"), sem("ws_masked")
        gu_ready, sv_ready, go_ready, gu_gelu, m_hi_done, sv_biased, m_done, m_lo_done, go_added = (
            sem(n) for n in ("gu_ready", "sv_ready", "go_ready", "gu_gelu", "m_hi_done", "sv_biased", "m_done",
                             "m_lo_done", "go_added"))
        vn_centred, vn_scaled, vn_done = sem("vn_centred"), sem("vn_scaled"), sem("vn_done")
        out_stored = [sem(f"out_stored_{s}") for s in range(2)]

        def wait(eng, s, value):
            if not isinstance(value, int) or value > 0:
                eng.wait_ge(s, value)

        def ring(main, more, at, n):
            return main[:, at:at + n] if at < RING else more[:, at - RING:at - RING + n]

        def w_hi(at, n):
            return ring(w_hi_main, w_hi_more, at, n)

        def w_lo(at, n):
            return ring(w_lo_main, w_lo_more, at, n)

        def f32(ap):
            return ap.bitcast(F32)

        def k4(ap):
            return ap.rearrange("p (k t) -> p k t", k=4)

        def tile(t):
            return slice(t * P, (t + 1) * P)

        def half(h):
            return slice(h * BANK, (h + 1) * BANK)

        def of(i, per, k):
            return i * per + k

        def at_gla(m, k):
            return (m % 2) * 8 * BANK + k * BANK

        def at_ffn(b):
            return b * BANK

        def at_gv(b):
            return b * GC

        def at_gp(b):
            return b * GC if b < 8 else 8 * GC + (b - 8) * BANK

        def src_gla(m, k):
            rows = slice(k * P, (k + 1) * P)
            col = [0, o_v, o_k, o_v + BANK, o_g, o_g + BANK][m] if m < 6 else (m - 6) * BANK
            return (a_w_in if m < 6 else a_w_out)[0, rows, col:col + BANK]

        def src_ffn(layer, i, b):
            if b < 8:
                cols = bass.ds(i * FC, FC)
                return [(0, FC, w_ffn_gate[layer, b * P:(b + 1) * P, cols]),
                        (FC, FC, w_ffn_up[layer, b * P:(b + 1) * P, cols])]
            kt, ch = (b - 8) // 2, (b - 8) % 2
            return [(0, BANK, w_ffn_down[layer, bass.ds(i * FC + kt * P, P), half(ch)])]

        def src_gv(i, b):
            g = i * 2 + b // 8
            return [(0, GC, b_w_in[0, (b % 8) * P:(b % 8 + 1) * P, bass.ds(g * GC + E, GC)])]

        def src_gp(g, b):
            if b < 8:
                return [(0, GC, b_w_in[0, b * P:(b + 1) * P, bass.ds(g * GC, GC)])]
            kt, ch = (b - 8) // 2, (b - 8) % 2
            return [(0, BANK, b_w_out[0, bass.ds(g * GC + kt * P, P), half(ch)])]

        def src(name, i, b):
            if name == "gla":
                return [(0, BANK, src_gla(b // 8, b % 8))]
            if name == "gv":
                return src_gv(i, b)
            if name == "gp":
                return src_gp(i, b)
            return src_ffn(int(name[-1]), i, b)

        def place(name, b):
            if name == "gla":
                return at_gla(b // 8, b % 8), BANK
            if name == "gv":
                return at_gv(b), GC
            if name == "gp":
                return at_gp(b), (GC if b < 8 else BANK)
            return at_ffn(b), BANK

        def load_block(sp, name, i, b):
            slot, _, _, before = blocks.at(name, i, b)
            wait(sp, w_lo_done, before)
            for col, n, source in src(name, i, b):
                sp.dma_start(stage[:, slot, col:col + n], source).then_inc(staged[slot], 16)

        def gla_used(m):
            if m < 4:
                return proj_ready, 8 * (m + 1)
            return (g_ready, 2 * NC - 5 + m) if m < 6 else (ao_ready, TT * (m - 5))

        def cut_hi(act, name, i, b, used):
            slot, landed, _, _ = blocks.at(name, i, b)
            at, n = place(name, b)
            wait(act, staged[slot], landed)
            if used is not None:
                wait(act, used[0], used[1])
            nc.scalar.activation(w_hi(at, n), stage[:, slot, 0:n], ACT.Copy).then_inc(w_hi_done, 1)

        def cut_lo(pool, name, i, b):
            slot, _, count, _ = blocks.at(name, i, b)
            at, n = place(name, b)
            wait(pool, w_hi_done, count)
            nc.gpsimd.tensor_tensor(w_lo(at, n), stage[:, slot, 0:n], f32(w_hi(at, n)),
                                    ALU.subtract).then_inc(w_lo_done, 1)

        def block_cut(pe, name, i, b):
            wait(pe, w_lo_done, blocks.at(name, i, b)[2])

        def product(pe, bank, s_hi, s_lo, m_hi_, m_lo_, k, last):
            pe.matmul(bank, s_hi, m_hi_, start=(k == 0), stop=False)
            pe.matmul(bank, s_hi, m_lo_, start=False, stop=False)
            return pe.matmul(bank, s_lo, m_hi_, start=False, stop=last)

        def norm_square(act, n, t, source, slot):
            nc.scalar.activation(slot, source, ACT.Square,
                                 accum_out=stats[:, n, 0, t:t + 1]).then_inc(squared[n], 1)
            act.wait_ge(squared[n], t + 1)
            nc.scalar.activation(stats[:, n, 1, t:t + 1], stats[:, n, 0, t:t + 1], ACT.Sqrt,
                                 bias=eps_col[:, 0:1], scale=1.0 / D).then_inc(rooted[n], 1)

        def norm_apply(dve, n, t, source, slot):
            dve.wait_ge(rooted[n], t + 1)
            nc.vector.reciprocal(stats[:, n, 2, t:t + 1], stats[:, n, 1, t:t + 1]).then_inc(inverted[n], 1)
            dve.wait_ge(inverted[n], t + 1)
            dve.wait_ge(gain_ld, 16 * (n + 1))
            nc.vector.scalar_tensor_tensor(out=slot, in0=source, scalar=stats[:, n, 2, t:t + 1], in1=gain_bc[:, :],
                                           op0=ALU.mult, op1=ALU.mult).then_inc(normed[n], 1)

        def norm_turn(pe, n, t, slot):
            pe.wait_ge(normed[n], t + 1)
            wait(pe, x_lo_done[n], 2 * t)
            for k in range(KT):
                mm = pe.transpose(ps[:, 1 + 2 * (k // 4), tile(k % 4)], slot[:, tile(k)], ident[:, :])
                if k % 4 == 3:
                    mm.then_inc(turned[n], 1)

        def norm_hi(act, n, t):
            for b in range(2):
                act.wait_ge(turned[n], 2 * t + b + 1)
                nc.scalar.activation(x_hi[:, 4 * b:4 * b + 4, tile(t)], k4(ps[:, 1 + 2 * b, :]),
                                     ACT.Copy).then_inc(x_hi_done[n], 1)

        def norm_lo(dve, n, t):
            for b in range(2):
                dve.wait_ge(x_hi_done[n], 2 * t + b + 1)
                nc.vector.tensor_tensor(x_lo[:, 4 * b:4 * b + 4, tile(t)], k4(ps[:, 1 + 2 * b, :]),
                                        f32(x_hi[:, 4 * b:4 * b + 4, tile(t)]),
                                        ALU.subtract).then_inc(x_lo_done[n], 1)

        def level(ap, b):
            return ap.rearrange("p (m two b) -> p m two b", two=2, b=b)

        qk_flat = qk[:, :, :].rearrange("p h t -> p (h t)")
        q_all, k_all = qk_flat[:, 0:H * CH], qk_flat[:, H * CH:2 * H * CH]
        NL = len(LEVELS)
        NC = S // CH
        vb, vg, v_bias = vn[:, 0:2, :], vn[:, 2:6, :], vn[:, 6:8, :]

        def loop(eng, n, body):
            body(0, False)
            with eng.Fori(1, n - 1) as i:
                body(i, False)
            body(n - 1, True)

        block = top.enter_context(nc.Block())

        @block.sync
        def _(sp):
            sp.dma_start(x_in[:, 0, :], x_d[0]).then_inc(x_ld[0], 16)
            sp.dma_start(gain_bc[:, :], norm_mix[0].partition_broadcast(P)).then_inc(gain_ld, 16)
            sp.dma_start(x_in[:, 1, :], x_d[1]).then_inc(x_ld[1], 16)
            sp.dma_start(ident[:, :], identity).then_inc(const_ld, 16)
            for b in range(4):
                load_block(sp, "gla", 0, b)
            for t in range(2, TT):
                sp.wait_ge(normed[0], t - 1)
                sp.dma_start(x_in[:, t % 2, :], x_d[t]).then_inc(x_ld[t % 2], 16)
                if t < 4:
                    load_block(sp, "gla", 0, 2 * t)
                    load_block(sp, "gla", 0, 2 * t + 1)
            sp.dma_start(wa_stage[:, :, :], a_w_in[0, :, o_a:o_a + RANK].rearrange("(k p) r -> p k r", p=P)
                         ).then_inc(wa_ld, 16)
            sp.dma_start(mask_stage[:, :, :], level_masks).then_inc(const_ld, 16)
            sp.dma_start(causal[:, :], causal_matrix).then_inc(const_ld, 16)
            sp.dma_start(gnorm_bc[:, :], a_g_norm[0].partition_broadcast(P)).then_inc(const_ld, 16)
            sp.dma_start(w_gate2[:, :], a_w_gate2[0]).then_inc(const_ld, 16)
            sp.dma_start(b_gate[:, :], a_b_gate).then_inc(const_ld, 16)

            def chunk_loads(col, which):
                cols = bass.ds(col, CH)
                if which == "al":
                    sp.dma_start(al_c[:, :], al_d[:, cols]).then_inc(al_ld, 16)
                elif which == "xc":
                    sp.dma_start(f32(xc_hi[:, :, :]), f32(x_hi[:, :, cols])).then_inc(xc_ld, 16)
                    sp.dma_start(f32(xc_lo[:, :, :]), f32(x_lo[:, :, cols])).then_inc(xc_ld, 16)
                elif which == "qk":
                    sp.dma_start(qk[:, :, :], qk_d[:, :, cols].rearrange("h p t -> p h t")).then_inc(qk_ld, 16)
                else:
                    sp.dma_start(v_sb[:, :], v_d[cols, :]).then_inc(v_ld, 16)

            for m in range(4):
                if m == 2:
                    sp.wait_ge(al_copied, HALVES)
                    sp.dma_start(al_d, al_sb[:, :]).then_inc(al_stored, 16)
                if m == 3:
                    sp.wait_ge(turned[0], 2 * TT)
                    sp.wait_ge(x_lo_done[0], 2 * TT)
                    sp.wait_ge(al_stored, 16)
                    chunk_loads(0, "al")
                    chunk_loads(0, "xc")
                for j in range(8):
                    if j < 4:
                        load_block(sp, "gla", 0, 8 * (m + 1) + 2 * j)
                        load_block(sp, "gla", 0, 8 * (m + 1) + 2 * j + 1)
                    q = 8 * m + j
                    if m % 2 == 0:
                        sp.wait_ge(qk_copied, 8 * (m // 2) + j + 1)
                        dst = qk_d[(m // 2) * H + j % H, :, half(j // H)]
                    else:
                        sp.wait_ge(v_copied, 8 * (m // 2) + j + 1)
                        dst = v_d[tile(j), half(m // 2)]
                    sp.dma_start(dst, evac[:, q % 4, :]).then_inc(evac_stored[q % 4], 16)
                    if q == 25:
                        for s in range(4):
                            sp.wait_ge(evac_stored[s], 16 * 6)
                        chunk_loads(0, "qk")
            for s in range(4):
                sp.wait_ge(evac_stored[s], 16 * 8)
            chunk_loads(0, "v")
            for b in range(8):
                load_block(sp, "gla", 0, 40 + b)

            def at(value):
                return value if isinstance(value, int) else sp.snap(value)

            def move_y(c, col):
                sp.wait_ge(y_lo_done, of(c, 2, 2))
                cols = bass.ds(col, CH)
                sp.dma_start(f32(x_hi[:, :, cols]), f32(y_hi[:, :, :])).then_inc(y_moved, 16)
                sp.dma_start(f32(x_lo[:, :, cols]), f32(y_lo[:, :, :])).then_inc(y_moved, 16)

            def chunk(c, last):
                before, after = at((c - 1) * CH), at((c + 1) * CH)
                if not isinstance(c, int) or c > 0:
                    move_y(c - 1, before)
                if not last:
                    sp.wait_ge(g_ready, of(c, 2, 2))
                    if not isinstance(c, int) or c < NC - 2:
                        chunk_loads((c + 2) * CH, "al")
                    chunk_loads(after, "xc")
                    sp.wait_ge(qk_decayed, of(c, 2, 2))
                    sp.wait_ge(z_done, of(c, NL, NL))
                    sp.wait_ge(level_ready, of(c, NL + 1, 1))
                    chunk_loads(after, "qk")
                    sp.wait_ge(s_ready, of(c, 2, 2))
                    chunk_loads(after, "v")

            def residual(t):
                sp.dma_start(resid[:, t, :], x_d[t]).then_inc(xr_ld[t // 3 > 0], 16)

            sp.wait_ge(z_ready, 1)
            chunk_loads(CH, "al")
            chunk(0, False)
            with sp.Fori(1, NC - 2) as c:
                chunk(c, False)
            chunk(NC - 2, False)
            chunk(NC - 1, True)
            for b in range(48, 52):
                load_block(sp, "gla", 0, b)
            sp.wait_ge(g_ready, 2 * NC)
            residual(0)
            residual(1)
            sp.wait_ge(qk_decayed, 2 * NC - 1)
            sp.wait_ge(z_done, NL * NC)
            sp.wait_ge(level_ready, (NL + 1) * (NC - 1) + 1)
            residual(2)
            for b in range(52, 56):
                load_block(sp, "gla", 0, b)
            sp.wait_ge(o_ready, 2 * NC)
            for t in range(3, TT):
                residual(t)
            for b in range(56, 60):
                load_block(sp, "gla", 0, b)
            move_y(NC - 1, (NC - 1) * CH)
            for b in range(60, 64):
                load_block(sp, "gla", 0, b)
            sp.wait_ge(normed[0], TT)
            sp.dma_start(gain_bc[:, :], norm_ffn[0].partition_broadcast(P)).then_inc(gain_ld, 16)
            for b in range(8):
                load_block(sp, "ffn0", 0, b)

            def ffn_loads(layer):
                name = f"ffn{layer}"

                def step(i, last):
                    for b in range(8, 12):
                        load_block(sp, name, i, b)
                    if not last:
                        for b in range(8):
                            load_block(sp, name, i + 1, b)
                loop(sp, FSTEPS, step)

            sp.wait_ge(normed[1], TT)
            sp.dma_start(gain_bc[:, :], norm_mix[1].partition_broadcast(P)).then_inc(gain_ld, 16)
            ffn_loads(0)
            for b in range(8):
                load_block(sp, "gv", 0, b)
            for s in range(2):
                sp.wait_ge(fsem[0]["down_ready"], 16 * FSTEPS)
                sp.dma_start(v_bias[:, s, :], b_b_in[0, E + s * GC:E + (s + 1) * GC].partition_broadcast(P)
                             ).then_inc(bias_ld[s], 16)

            def gv(i, last):
                for par in range(2):
                    for j in range(4):
                        if par == 0:
                            load_block(sp, "gv", i, 8 + 2 * j)
                            load_block(sp, "gv", i, 8 + 2 * j + 1)
                        elif not last:
                            load_block(sp, "gv", i + 1, 2 * j)
                            load_block(sp, "gv", i + 1, 2 * j + 1)
                        else:
                            load_block(sp, "gp", 0, 2 * j)
                            load_block(sp, "gp", 0, 2 * j + 1)
                        for t in (2 * j, 2 * j + 1):
                            sp.wait_ge(gv_gelu, of(i, 16, 8 * par + t + 1))
                            sp.dma_start(u_d[bass.ds(i * 2 + par, 1), t, :, :].rearrange("g p c -> p (g c)"),
                                         vg[:, t % 4, :]).then_inc(gv_stored[t % 4], 16)
                    if not last:
                        sp.wait_ge(gv_biased, of(i, 16, 8 * par + 8))
                        sp.dma_start(v_bias[:, par, :],
                                     b_b_in[0, bass.ds((i + 1) * (2 * GC) + (E + par * GC), GC)].partition_broadcast(P)
                                     ).then_inc(bias_ld[par], 16)

            loop(sp, G // 2, gv)
            sp.wait_ge(normed[2], TT)
            sp.dma_start(gain_bc[:, :], norm_ffn[1].partition_broadcast(P)).then_inc(gain_ld, 16)

            def group_loads(g):
                small_loads(g)
                v_loads(g)

            def small_loads(g):
                sp.dma_start(ws_raw[:, :], b_w_s[0, bass.ds(g, 1)].rearrange("g t s -> t (g s)")).then_inc(ws_ld, 16)
                sp.dma_start(b_u[:, :], b_b_in[0, bass.ds(g * GC, GC)].rearrange("(e p) -> p e", p=P),
                             allow_slow_non_contiguous=True).then_inc(bu_ld, 16)
                sp.dma_start(bs_bc[:, :], b_b_s[0, bass.ds(g, 1)].rearrange("g t -> (g t)").partition_broadcast(P)
                             ).then_inc(bu_ld, 16)

            def v_loads(g):
                for t in range(TT):
                    sp.dma_start(vn[:, t, :], u_d[bass.ds(g, 1), t, :, :].rearrange("g p c -> p (g c)")
                                 ).then_inc(vn_ld, 16)
                wait(sp, vn_done, of(g, TT, 0))
                cols = bass.ds(g * GC, GC)
                sp.dma_start(ln_g_bc[:, :], b_ln_g[0, cols].partition_broadcast(P)).then_inc(ln_ld, 16)
                sp.dma_start(ln_b_bc[:, :], b_ln_b[0, cols].partition_broadcast(P)).then_inc(ln_ld, 16)

            small_loads(0)
            for s in range(4):
                sp.wait_ge(gv_stored[s], 16 * G * TT // 4)
            sp.wait_ge(mv_done, TT)
            v_loads(0)

            def gp(g, last):
                for b in range(8, 14):
                    load_block(sp, "gp", g, b)
                if not last:
                    sp.wait_ge(sv_ready, of(g, 6, 6))
                    sp.wait_ge(gu_gelu, of(g, 6, 6))
                    sp.wait_ge(sv_biased, of(g, 6, 6))
                    group_loads(g + 1)
                    for b in range(8):
                        load_block(sp, "gp", g + 1, b)
                else:
                    for b in range(8):
                        load_block(sp, "ffn1", 0, b)

            loop(sp, G, gp)
            sp.wait_ge(normed[3], TT)
            sp.dma_start(gain_bc[:, :], norm_final.partition_broadcast(P)).then_inc(gain_ld, 16)
            ffn_loads(1)
            for t in range(TT):
                sp.wait_ge(normed[4], t + 1)
                sp.dma_start(out_d[t], work[:, t % 2, :]).then_inc(out_stored[t % 2], 16)
            for s in range(2):
                sp.wait_ge(out_stored[s], 16 * TT // 2)

        @block.gpsimd
        def _(pool):
            nc.gpsimd.memset(ones[:, :], 1.0).then_inc(consts_set, 1)
            nc.gpsimd.memset(eps_col[:, :], EPS).then_inc(consts_set, 1)
            for b in range(8):
                cut_lo(pool, "gla", 0, b)
            pool.wait_ge(wa_hi_done, 1)
            nc.gpsimd.tensor_tensor(wa_lo[:, :, :], wa_stage[:, :, :], f32(wa_hi[:, :, :]),
                                    ALU.subtract).then_inc(wa_lo_done, 1)
            for b in range(8, 40):
                cut_lo(pool, "gla", 0, b)

            def chunk(c, last):
                pool.wait_ge(bcum_done, c + 1)
                for n, b in enumerate(LEVELS):
                    bv, ev = level(bcum[:, :], b), level(ebuf[:, n % 2, :], b)
                    edge = bv[:, :, 0, b - 1:b].to_broadcast([P, H * CH // (2 * b), b])
                    wait(pool, z_done, of(c, NL, max(n - 1, 0)))
                    nc.gpsimd.tensor_tensor(ev[:, :, 1, :], bv[:, :, 1, :], edge, ALU.subtract)
                    nc.gpsimd.tensor_tensor(ev[:, :, 0, :], edge, bv[:, :, 0, :],
                                            ALU.subtract).then_inc(exponent_done, 1)
                    if n == 1 and isinstance(c, int) and c == 0:
                        for b5 in range(40, 48):
                            cut_lo(pool, "gla", 0, b5)
                pool.wait_ge(g_silu, of(c, 2, 2))
                gv_ = g_sb[:, :].rearrange("p (h e) -> p h e", h=H)
                for h in range(H):
                    gain = nc.gpsimd.tensor_tensor(gv_[:, h, :], gv_[:, h, :], gnorm_bc[:, :], ALU.mult)
                gain.then_inc(g_gained, 1)
                if last:
                    for b in range(48, 64):
                        cut_lo(pool, "gla", 0, b)

            pool.wait_ge(const_ld, 16 * 6)
            loop(pool, NC, chunk)
            for b in range(8):
                cut_lo(pool, "ffn0", 0, b)

            def ffn_cuts(layer, after):
                name = f"ffn{layer}"

                def step(i, last):
                    for b in range(8, 12):
                        cut_lo(pool, name, i, b)
                    for b in range(8):
                        if not last:
                            cut_lo(pool, name, i + 1, b)
                        elif after:
                            cut_lo(pool, after, 0, b)
                loop(pool, FSTEPS, step)

            ffn_cuts(0, "gv")

            def gv(i, last):
                for b in range(8, 16):
                    cut_lo(pool, "gv", i, b)
                for b in range(8):
                    if not last:
                        cut_lo(pool, "gv", i + 1, b)
                    else:
                        cut_lo(pool, "gp", 0, b)

            loop(pool, G // 2, gv)

            def scale_vn(g):
                pool.wait_ge(ln_ld, of(g, 32, 32))
                for t in range(TT):
                    pool.wait_ge(vn_centred, of(g, TT, t + 1))
                    nc.gpsimd.tensor_tensor(vn[:, t, :], vn[:, t, :], ln_g_bc[:, :], ALU.mult
                                            ).then_inc(vn_scaled, 1)
                    pool.wait_ge(vn_scaled, of(g, TT, t + 1))
                    nc.gpsimd.tensor_tensor(vn[:, t, :], vn[:, t, :], ln_b_bc[:, :], ALU.add
                                            ).then_inc(vn_done, 1)

            scale_vn(0)

            def gp(g, last):
                for b in range(8, 14):
                    cut_lo(pool, "gp", g, b)
                for b in range(8):
                    if not last:
                        cut_lo(pool, "gp", g + 1, b)
                    else:
                        cut_lo(pool, "ffn1", 0, b)
                if not last:
                    scale_vn(g + 1)

            loop(pool, G, gp)
            ffn_cuts(1, None)

        @block.scalar
        def _(act):
            act.wait_ge(consts_set, 2)
            for t in range(TT):
                act.wait_ge(x_ld[t % 2], 16 * (t // 2 + 1))
                wait(act, turned[0], 2 * (t - 1))
                norm_square(act, 0, t, x_in[:, t % 2, :], xn0[:, t % 2, :])
                if t < 4:
                    cut_hi(act, "gla", 0, 2 * t, None)
                    cut_hi(act, "gla", 0, 2 * t + 1, None)
                if t >= 1:
                    norm_hi(act, 0, t - 1)
            norm_hi(act, 0, TT - 1)
            act.wait_ge(wa_ld, 16)
            nc.scalar.activation(wa_hi[:, :, :], wa_stage[:, :, :], ACT.Copy).then_inc(wa_hi_done, 1)

            def exp_abs(c):
                act.wait_ge(z_ready, c + 1)
                wait(act, log_a_done, of(c, 1, 0))
                nc.scalar.activation(soft[:, :], ps[:, 2, :], ACT.Abs).then_inc(z_abs, 1)
                act.wait_ge(z_abs, c + 1)
                nc.scalar.activation(soft[:, :], soft[:, :], ACT.Exp, scale=-1.0).then_inc(z_exp, 1)

            def softplus(c):
                act.wait_ge(z_exp, c + 1)
                nc.scalar.activation(soft[:, :], soft[:, :], ACT.Ln, bias=1.0).then_inc(z_soft, 1)

            for m in range(4):
                for j in range(8):
                    if j < 4:
                        cut_hi(act, "gla", 0, 8 * (m + 1) + 2 * j, gla_used(m - 1) if m else None)
                        cut_hi(act, "gla", 0, 8 * (m + 1) + 2 * j + 1, gla_used(m - 1) if m else None)
                    if m % 2 == 0:
                        q = 8 * m + j
                        act.wait_ge(proj_ready, q + 1)
                        wait(act, evac_stored[q % 4], 16 * (q // 4))
                        nc.scalar.activation(evac[:, q % 4, :], ps[:, 4 + q % 4, :], ACT.Copy).then_inc(qk_copied, 1)
                    if m == 1 and j == 0:
                        for h in range(HALVES):
                            act.wait_ge(al_ready, h + 1)
                            nc.scalar.activation(al_sb[:, half(h)], ps[0:RANK, 2 * h, :], ACT.Copy
                                                 ).then_inc(al_copied, 1)
            act.wait_ge(al_ld, 16)
            exp_abs(0)
            softplus(0)

            def turn_hi(c):
                wait(act, y_moved, of(c, 32, 0))
                for b in range(2):
                    act.wait_ge(y_turned, of(c, 2, b + 1))
                    nc.scalar.activation(y_hi[:, 4 * b:4 * b + 4, :], k4(ps[:, 6 + b, :]), ACT.Copy
                                         ).then_inc(y_hi_done, 1)

            def cumulated(c):
                act.wait_ge(cum_ready, c + 1)
                wait(act, exponent_done, of(c, NL, 0))
                nc.scalar.activation(bcum[:, :], ps[:, 3, :], ACT.Copy, scale=1.0 / GLA_TAU).then_inc(bcum_done, 1)

            def chunk(c, last):
                first = isinstance(c, int) and c == 0

                def expo(n):
                    act.wait_ge(exponent_done, of(c, NL, n + 1))
                    nc.scalar.activation(ebuf[:, n % 2, :], ebuf[:, n % 2, :], ACT.Exp).then_inc(exp_done, 1)

                expo(0)
                expo(1)
                if first:
                    for b in range(8):
                        cut_hi(act, "gla", 0, 40 + b, gla_used(3))
                act.wait_ge(bcum_done, c + 1)
                wait(act, o_ready, of(c, 2, 0))
                nc.scalar.activation(q_dec[:, :, :], bcum[:, :].rearrange("p (h t) -> p h t", h=H), ACT.Exp
                                     ).then_inc(q_exp, 1)
                if not last:
                    exp_abs(c + 1)
                expo(2)
                if not first:
                    turn_hi(c - 1)
                if not last:
                    softplus(c + 1)
                expo(3)
                if not last:
                    wait(act, k_turned, of(c, 1, 0))
                    for h in range(H):
                        nc.scalar.activation(k_dec[:, h, :], bcum[:, tile(h)], ACT.Exp, scale=-1.0,
                                             bias=bcum[:, h * CH + CH - 1:h * CH + CH]).then_inc(k_exp, 1)
                    wait(act, state_done, of(c, H, 2))
                    nc.scalar.activation(eb_last[:, :], bcum[:, CH - 1::CH], ACT.Exp).then_inc(last_exp, 1)
                expo(4)
                expo(5)
                expo(6)
                if not last:
                    cumulated(c + 1)
                wait(act, y_turned, of(c, 2, 0))
                for b in range(2):
                    act.wait_ge(g_ready, of(c, 2, b + 1))
                    nc.scalar.activation(g_sb[:, half(b)], ps[:, b, :], ACT.Silu).then_inc(g_silu, 1)
                if not last:
                    act.wait_ge(k_turned, c + 1)
                    wait(act, s_ready, of(c, 2, 0))
                    nc.scalar.activation(k_dec_t[:, :, :], k4(ps[:, 2, :]), ACT.Copy).then_inc(k_dec_t_done, 1)
                    act.wait_ge(log_a_done, c + 2)
                else:
                    for b in range(48, 56):
                        cut_hi(act, "gla", 0, b, gla_used(4))
                for h in range(H):
                    act.wait_ge(o_ready, of(c, 2, h // 2 + 1))
                    nc.scalar.activation(soft[:, 0:DV], ps[:, 6 + h // 2, (h % 2) * DV:(h % 2 + 1) * DV],
                                         ACT.Square, accum_out=ostat[:, 0, h:h + 1]).then_inc(o_sq, 1)
                    act.wait_ge(o_sq, of(c, H, h + 1))
                nc.scalar.activation(ostat[:, 1, :], ostat[:, 0, :], ACT.Sqrt, bias=eps_col[:, 0:1],
                                     scale=1.0 / DV).then_inc(o_root, 1)

            for s in range(4):
                act.wait_ge(evac_stored[s], 16 * 8)
            cumulated(0)
            loop(act, NC, chunk)
            turn_hi(NC - 1)
            for b in range(56, 64):
                cut_hi(act, "gla", 0, b, gla_used(5))
            for t in range(TT + 2):
                if t < TT:
                    act.wait_ge(ao_added, TT + t + 1)
                    wait(act, turned[1], 2 * (t - 1))
                    norm_square(act, 1, t, resid[:, t, :], work[:, t % 2, :])
                    if t < 4:
                        cut_hi(act, "ffn0", 0, 2 * t, gla_used(6))
                        cut_hi(act, "ffn0", 0, 2 * t + 1, gla_used(6))
                if t >= 2:
                    norm_hi(act, 1, t - 2)

            def ffn_act(layer, n, after):
                s, name = fsem[layer], f"ffn{layer}"
                before = (go_ready, 16 * G) if layer else gla_used(7)

                def step(i, last):
                    for p in range(4):
                        hf, j = p // 2, p % 2
                        act.wait_ge(s["gate_ready"], of(i, 4, p + 1))
                        wait(act, s["prod_done"], of(i, 4, p - 1))
                        nc.scalar.activation(work[:, 0, half(p % 2)], ps[:, p % 2, :], ACT.Silu
                                             ).then_inc(s["silu_done"], 1)
                        cut_hi(act, name, i, 8 + p,
                               before if isinstance(i, int) and i == 0 else (s["down_ready"], of(i, 16, 0)))
                        act.wait_ge(s["prod_done"], of(i, 4, p + 1))
                        nc.scalar.activation(h_hi[:, j, half(hf)], prod[:, p % 2, :], ACT.Copy
                                             ).then_inc(s["h_hi_done"], 1)
                    if not last:
                        for b in range(8):
                            cut_hi(act, name, i + 1, b, (s["up_ready"], of(i, 4, 4)))
                        return
                    for t in range(TT + (2 if after else 0)):
                        if t < TT:
                            act.wait_ge(s["down_added"], 16 * i + 2 * t + 2)
                            if after:
                                wait(act, turned[n], 2 * (t - 1))
                                if t < 4:
                                    cut_hi(act, after, 0, 2 * t, (s["up_ready"], of(i, 4, 4)))
                                    cut_hi(act, after, 0, 2 * t + 1, (s["up_ready"], of(i, 4, 4)))
                            else:
                                wait(act, out_stored[t % 2], 16 * (t // 2))
                            norm_square(act, n, t, resid[:, t, :], work[:, t % 2, :])
                        if after and t >= 2:
                            norm_hi(act, n, t - 2)
                loop(act, FSTEPS, step)

            ffn_act(0, 2, "gv")

            def gv(i, last):
                for par in range(2):
                    for t in range(TT):
                        act.wait_ge(gv_biased, of(i, 16, 8 * par + t + 1))
                        wait(act, gv_stat, of(i, 16, 8 * par + t - 3))
                        q4 = 2 * par + t // 4
                        wait(act, gv_stored[t % 4], of(i, 64, 16 * q4))
                        nc.scalar.activation(vg[:, t % 4, :], vb[:, t % 2, :], ACT.Gelu_apprx_tanh
                                             ).then_inc(gv_gelu, 1)
                        free = (gv_ready, of(i, 16, 8 * par))
                        if par == 0 and isinstance(i, int) and i == 0:
                            free = (fsem[0]["down_ready"], 16 * FSTEPS)
                        if par == 0:
                            cut_hi(act, "gv", i, 8 + t, free)
                        elif not last:
                            cut_hi(act, "gv", i + 1, t, free)
                        else:
                            cut_hi(act, "gp", 0, t, free)

            loop(act, G // 2, gv)
            act.wait_ge(mv_done, TT)
            nc.scalar.activation(dev[:, :], mv[:, :, 1], ACT.Sqrt, bias=eps_col[:, 0:1]).then_inc(dev_done, 1)

            def gp(g, last):
                outputs_used = (go_ready, of(g, 16, 0)) if not isinstance(g, int) or g else (gv_ready, TT * G)
                act.wait_ge(bu_ld, of(g, 32, 32))
                for q in range(6):
                    hf, e = q // 3, q % 3
                    act.wait_ge(gu_ready, of(g, 6, q + 1))
                    wait(act, m_done, of(g, 6, q - 1))
                    nc.scalar.activation(work[:, 0, half(q % 2)], ps[:, q % 2, :], ACT.Gelu_apprx_tanh,
                                         bias=b_u[:, e:e + 1]).then_inc(gu_gelu, 1)
                    cut_hi(act, "gp", g, 8 + q, outputs_used)
                    act.wait_ge(m_done, of(g, 6, q + 1))
                    nc.scalar.activation(m_hi[:, e, half(hf)], work[:, 1, half(q % 2)], ACT.Copy
                                         ).then_inc(m_hi_done, 1)
                if not last:
                    for b in range(8):
                        cut_hi(act, "gp", g + 1, b, (gu_ready, of(g, 6, 6)))
                    return
                for t in range(TT + 2):
                    if t < TT:
                        act.wait_ge(go_added, 16 * g + 2 * t + 2)
                        wait(act, turned[3], 2 * (t - 1))
                        norm_square(act, 3, t, resid[:, t, :], work[:, t % 2, :])
                        if t < 3:
                            cut_hi(act, "ffn1", 0, 2 * t, (gu_ready, 6 * G))
                            cut_hi(act, "ffn1", 0, 2 * t + 1, (gu_ready, 6 * G))
                    if t == TT:
                        cut_hi(act, "ffn1", 0, 6, (go_ready, 16 * G))
                        cut_hi(act, "ffn1", 0, 7, (go_ready, 16 * G))
                    if t >= 2:
                        norm_hi(act, 3, t - 2)

            loop(act, G, gp)
            ffn_act(1, 4, None)

        @block.vector
        def _(dve):
            for t in range(TT):
                norm_apply(dve, 0, t, x_in[:, t % 2, :], xn0[:, t % 2, :])
                if t >= 1:
                    norm_lo(dve, 0, t - 1)
            norm_lo(dve, 0, TT - 1)
            dve.wait_ge(const_ld, 16 * 6)
            nc.vector.tensor_copy(masks[:, :, :], mask_stage[:, :, :]).then_inc(masks_made, 1)

            def log_sigmoid(c):
                dve.wait_ge(z_soft, c + 1)
                wait(dve, cum_ready, of(c, 1, 0))
                nc.vector.scalar_tensor_tensor(out=log_a[:, :], in0=ps[:, 2, :], scalar=0.0, in1=soft[:, :],
                                               op0=ALU.min, op1=ALU.subtract).then_inc(log_a_done, 1)

            def scale_q(c):
                dve.wait_ge(qk_ld, of(c, 16, 16))
                nc.vector.tensor_scalar(q_all, q_all, float(DK) ** -0.5, None, ALU.mult).then_inc(q_scaled, 1)

            for m in (1, 3):
                for j in range(8):
                    q = 8 * m + j
                    dve.wait_ge(proj_ready, q + 1)
                    dve.wait_ge(evac_stored[q % 4], 16 * (q // 4))
                    nc.vector.tensor_copy(evac[:, q % 4, :], ps[:, 4 + q % 4, :]).then_inc(v_copied, 1)
                    if m == 3 and j == 6:
                        log_sigmoid(0)
            dve.wait_ge(masks_made, 1)
            nc.vector.memset(state[:, :, :], 0.0).then_inc(state_done, 1)
            nc.vector.memset(att[:, :, :], 0.0).then_inc(state_done, 1)
            dve.wait_ge(state_done, 2)
            scale_q(0)

            def turn_lo(c):
                for b in range(2):
                    dve.wait_ge(y_hi_done, of(c, 2, b + 1))
                    nc.vector.tensor_tensor(y_lo[:, 4 * b:4 * b + 4, :], k4(ps[:, 6 + b, :]),
                                            f32(y_hi[:, 4 * b:4 * b + 4, :]), ALU.subtract).then_inc(y_lo_done, 1)

            def chunk(c, last):
                first = isinstance(c, int) and c == 0
                dve.wait_ge(q_scaled, c + 1)

                def keep(n):
                    dve.wait_ge(level_ready, of(c, NL + 1, n + 1))
                    if n == 0:
                        wait(dve, o_ready, of(c, 2, 0))
                    else:
                        dve.wait_ge(level_kept, of(c, NL + 1, n))
                    nc.vector.tensor_copy(tick[:, :], eps_col[:, :])
                    nc.vector.copy_predicated(att[:, :, :], masks[:, n:n + 1, :].to_broadcast([P, H, CH]),
                                              k4(ps[:, 4 + n % 2, :])).then_inc(level_kept, 1)

                for n, b in enumerate(LEVELS):
                    dve.wait_ge(exp_done, of(c, NL, n + 1))
                    if n >= 2:
                        dve.wait_ge(level_ready, of(c, NL + 1, n))
                    else:
                        wait(dve, level_ready, of(c, NL + 1, 0))
                    ev, zv = level(ebuf[:, n % 2, :], b), level(zbuf[:, n % 2, :], b)
                    nc.vector.tensor_tensor(zv[:, :, 1, :], ev[:, :, 1, :], level(q_all, b)[:, :, 1, :], ALU.mult)
                    nc.vector.tensor_tensor(zv[:, :, 0, :], ev[:, :, 0, :], level(k_all, b)[:, :, 0, :],
                                            ALU.mult).then_inc(z_done, 1)
                    keep(n)
                    if n == 2:
                        if not first:
                            turn_lo(c - 1)
                        if not last:
                            log_sigmoid(c + 1)
                    if n == 4:
                        dve.wait_ge(q_exp, c + 1)
                        nc.vector.tensor_tensor(q_dec[:, :, :], q_dec[:, :, :], qk[:, 0:H, :], ALU.mult
                                                ).then_inc(qk_decayed, 1)
                        if not last:
                            dve.wait_ge(k_exp, of(c, H, H))
                            nc.vector.tensor_tensor(k_dec[:, :, :], k_dec[:, :, :], qk[:, H:2 * H, :], ALU.mult
                                                    ).then_inc(qk_decayed, 1)
                keep(NL)
                if not last:
                    scale_q(c + 1)
                    dve.wait_ge(last_exp, c + 1)
                    for h in range(H):
                        dve.wait_ge(s_ready, of(c, 2, h // 2 + 1))
                        nc.vector.scalar_tensor_tensor(
                            out=state[:, h, :], in0=state[:, h, :], scalar=eb_last[:, h:h + 1],
                            in1=ps[:, 3 - h // 2, (h % 2) * DV:(h % 2 + 1) * DV], op0=ALU.mult, op1=ALU.add
                        ).then_inc(state_done, 1)
                dve.wait_ge(o_root, c + 1)
                nc.vector.reciprocal(ostat[:, 2, :], ostat[:, 1, :]).then_inc(o_inv, 1)
                dve.wait_ge(o_inv, c + 1)
                dve.wait_ge(g_gained, c + 1)
                for h in range(H):
                    y = nc.vector.scalar_tensor_tensor(
                        out=g_sb[:, h * DV:(h + 1) * DV], in0=ps[:, 6 + h // 2, (h % 2) * DV:(h % 2 + 1) * DV],
                        scalar=ostat[:, 2, h:h + 1], in1=g_sb[:, h * DV:(h + 1) * DV], op0=ALU.mult, op1=ALU.mult)
                y.then_inc(y_done, 1)

            loop(dve, NC, chunk)
            for q in range(2 * TT):
                t, ch = q % TT, q // TT
                dve.wait_ge(ao_ready, q + 1)
                if q == 0:
                    dve.wait_ge(xr_ld[0], 16 * 3)
                if q == 3:
                    dve.wait_ge(xr_ld[1], 16 * (TT - 3))
                nc.vector.tensor_tensor(resid[:, t, half(ch)], resid[:, t, half(ch)], ps[:, 4 + q % 4, :], ALU.add
                                        ).then_inc(ao_added, 1)
                if q == 0:
                    turn_lo(NC - 1)
                if ch and t >= 1:
                    norm_apply(dve, 1, t - 1, resid[:, t - 1, :], work[:, (t - 1) % 2, :])
                if ch and t >= 2:
                    norm_lo(dve, 1, t - 2)
            norm_apply(dve, 1, TT - 1, resid[:, TT - 1, :], work[:, (TT - 1) % 2, :])
            norm_lo(dve, 1, TT - 2)
            norm_lo(dve, 1, TT - 1)

            def add_down(i, ready, added, n, turned_too, behind=None):
                for t in range(TT):
                    for ch in range(2):
                        q = 2 * t + ch
                        dve.wait_ge(ready, of(i, 16, q + 1))
                        nc.vector.tensor_tensor(resid[:, t, half(ch)], resid[:, t, half(ch)], ps[:, 4 + q % 4, :],
                                                ALU.add).then_inc(added, 1)
                    if behind is not None and t >= 4:
                        behind(t)
                    if n is not None:
                        if t >= 1:
                            norm_apply(dve, n, t - 1, resid[:, t - 1, :], work[:, (t - 1) % 2, :])
                        if t >= 2 and turned_too:
                            norm_lo(dve, n, t - 2)
                if n is not None:
                    norm_apply(dve, n, TT - 1, resid[:, TT - 1, :], work[:, (TT - 1) % 2, :])
                    if turned_too:
                        norm_lo(dve, n, TT - 2)
                        norm_lo(dve, n, TT - 1)

            def ffn_dve(layer, n):
                s = fsem[layer]

                def step(i, last):
                    for p in range(4):
                        hf, j = p // 2, p % 2
                        dve.wait_ge(s["silu_done"], of(i, 4, p + 1))
                        dve.wait_ge(s["up_ready"], of(i, 4, p + 1))
                        wait(dve, s["h_hi_done"], of(i, 4, p - 1))
                        nc.vector.tensor_tensor(prod[:, p % 2, :], work[:, 0, half(p % 2)], ps[:, 2 + p % 2, :],
                                                ALU.mult).then_inc(s["prod_done"], 1)
                        dve.wait_ge(s["h_hi_done"], of(i, 4, p + 1))
                        nc.vector.tensor_tensor(h_lo[:, j, half(hf)], prod[:, p % 2, :],
                                                f32(h_hi[:, j, half(hf)]), ALU.subtract).then_inc(s["h_lo_done"], 1)
                    add_down(i, s["down_ready"], s["down_added"], n if last else None, n != 4)
                loop(dve, FSTEPS, step)

            ffn_dve(0, 2)

            def gv(i, last):
                def stat(par, t):
                    dve.wait_ge(gv_gelu, of(i, 16, 8 * par + t + 1))
                    nc.vector.bn_stats(st6[:, t, :], vg[:, t % 4, :]).then_inc(gv_stat, 1)

                for par in range(2):
                    dve.wait_ge(bias_ld[par], of(i, 16, 16))
                    for t in range(TT):
                        dve.wait_ge(gv_ready, of(i, 16, 8 * par + t + 1))
                        wait(dve, gv_gelu, of(i, 16, 8 * par + t - 1))
                        nc.vector.tensor_tensor(vb[:, t % 2, :], ps[:, 4 + t % 4, 0:GC], v_bias[:, par, :], ALU.add
                                                ).then_inc(gv_biased, 1)
                        if t == 0:
                            wait(dve, gv_kept, of(i, 2, par))
                        if t >= 1:
                            stat(par, t - 1)
                    stat(par, TT - 1)
                    dve.wait_ge(gv_stat, of(i, 16, 8 * par + 8))
                    nc.vector.tensor_scalar(st_all[:, :, bass.ds(i * 2 + par, 1), :],
                                            st6[:, :, :].rearrange("p t (g s) -> p t g s", g=1), 1.0, None, ALU.mult
                                            ).then_inc(gv_kept, 1)

            loop(dve, G // 2, gv)
            dve.wait_ge(gv_kept, G)
            for t in range(TT):
                nc.vector.bn_aggr(mv[:, t, :], st_all[:, t, :, :].rearrange("p g s -> p (g s)")).then_inc(mv_done, 1)
            dve.wait_ge(dev_done, 1)
            nc.vector.reciprocal(dev[:, :], dev[:, :]).then_inc(inv_done, 1)
            dve.wait_ge(inv_done, 1)

            def centre(g, t0, n):
                if t0 == 0:
                    dve.wait_ge(vn_ld, of(g, 16 * TT, 16 * TT))
                for t in range(t0, t0 + n):
                    nc.vector.tensor_scalar(vn[:, t, :], vn[:, t, :], mv[:, t, 0:1], dev[:, t:t + 1], ALU.subtract,
                                            ALU.mult).then_inc(vn_centred, 1)

            centre(0, 0, TT)

            def gp(g, last):
                dve.wait_ge(ws_turned, g + 1)
                wait(dve, sv_ready, of(g, 6, 0))
                nc.vector.tensor_tensor(ws_t[:, :], ps[:, 1, 0:P], causal[:, :], ALU.mult).then_inc(ws_masked, 1)
                dve.wait_ge(bu_ld, of(g, 32, 32))
                for q in range(6):
                    hf, e = q // 3, q % 3
                    t1 = work[:, 1, half(q % 2)]
                    dve.wait_ge(sv_ready, of(g, 6, q + 1))
                    wait(dve, m_hi_done, of(g, 6, q - 1))
                    nc.vector.tensor_tensor(k4(t1), k4(ps[:, 2 + q % 2, :]),
                                            bs_bc[:, :].rearrange("p (o t) -> p o t", o=1).to_broadcast([P, 4, P]),
                                            ALU.add).then_inc(sv_biased, 1)
                    dve.wait_ge(sv_biased, of(g, 6, q + 1))
                    dve.wait_ge(gu_gelu, of(g, 6, q + 1))
                    nc.vector.tensor_tensor(t1, t1, work[:, 0, half(q % 2)], ALU.mult).then_inc(m_done, 1)
                    dve.wait_ge(m_hi_done, of(g, 6, q + 1))
                    nc.vector.tensor_tensor(m_lo[:, e, half(hf)], t1, f32(m_hi[:, e, half(hf)]), ALU.subtract
                                            ).then_inc(m_lo_done, 1)

                def centre_two(t):
                    centre(g + 1, 2 * (t - 4), 2)

                add_down(g, go_ready, go_added, 3 if last else None, True, None if last else centre_two)

            loop(dve, G, gp)
            ffn_dve(1, 4)

        @block.tensor
        def _(pe):
            pe.wait_ge(const_ld, 16)
            for t in range(TT // 2):
                norm_turn(pe, 0, t, xn0[:, t % 2, :])
            pe.wait_ge(x_lo_done[0], TT)

            def gate_logits(c):
                pe.wait_ge(al_ld, of(c, 16, 16))
                if not isinstance(c, int) or c > 0:
                    pe.wait_ge(state_done, of(c, H, 2 - H))
                pe.matmul(ps[:, 2, :], al_c[:, :], w_gate2[:, :], start=True, stop=False)
                pe.matmul(ps[:, 2, :], ones[:, :], b_gate[:, :], start=False, stop=True).then_inc(z_ready, 1)

            def cumulate(c):
                pe.wait_ge(log_a_done, c + 1)
                for h in range(H):
                    mm = pe.matmul(ps[:, 3, tile(h)], log_a[:, tile(h)], causal[:, :], start=True, stop=True)
                mm.then_inc(cum_ready, 1)

            for m in range(4):
                if m == 1:
                    pe.wait_ge(wa_lo_done, 1)
                    for h in range(HALVES):
                        for k in range(KT):
                            mm = product(pe, ps[0:RANK, 2 * h, :], wa_hi[:, k, :], wa_lo[:, k, :],
                                         x_hi[:, k, half(h)], x_lo[:, k, half(h)], k, k == KT - 1)
                        mm.then_inc(al_ready, 1)
                for j in range(8):
                    q = 8 * m + j
                    if q == 4:
                        pe.wait_ge(x_lo_done[0], 2 * TT)
                    if q == 28:
                        pe.wait_ge(const_ld, 16 * 6)
                        pe.wait_ge(consts_set, 2)
                        gate_logits(0)
                    if j < 4 and m:
                        wait(pe, qk_copied if m % 2 else v_copied, 8 * ((m - 1) // 2) + j + 5)
                    elif j >= 4:
                        wait(pe, v_copied if m % 2 else qk_copied, 8 * (m // 2) + j - 3)
                    for k in range(KT):
                        if j == 0:
                            block_cut(pe, "gla", 0, 8 * m + k)
                        at = at_gla(m, k)
                        if m % 2 == 0:
                            col = at + (j % H) * P
                            mm = product(pe, ps[:, 4 + q % 4, :], w_hi(col, P), w_lo(col, P),
                                         x_hi[:, k, half(j // H)], x_lo[:, k, half(j // H)], k, k == KT - 1)
                        else:
                            pe_s = (x_hi[:, k, tile(j)], x_lo[:, k, tile(j)])
                            pe.matmul(ps[:, 4 + q % 4, :], pe_s[0], w_hi(at, BANK), start=(k == 0), stop=False)
                            pe.matmul(ps[:, 4 + q % 4, :], pe_s[0], w_lo(at, BANK), start=False, stop=False)
                            mm = pe.matmul(ps[:, 4 + q % 4, :], pe_s[1], w_hi(at, BANK), start=False,
                                           stop=(k == KT - 1))
                    mm.then_inc(proj_ready, 1)
                    if q < 4:
                        norm_turn(pe, 0, 4 + q, xn0[:, q % 2, :])
            cumulate(0)
            pe.wait_ge(state_done, 2)

            def turn_y(c):
                pe.wait_ge(y_done, c + 1)
                for k in range(KT):
                    mm = pe.transpose(ps[:, 6 + k // 4, tile(k % 4)], g_sb[:, tile(k)], ident[:, :])
                    if k % 4 == 3:
                        mm.then_inc(y_turned, 1)

            def chunk(c, last):
                first = isinstance(c, int) and c == 0

                def gate(b, k0, k1):
                    if b == 0:
                        pe.wait_ge(xc_ld, of(c, 32, 32))
                    if k0 == 0:
                        wait(pe, g_silu, of(c, 2, b - 1))
                    for k in range(k0, k1):
                        if first:
                            block_cut(pe, "gla", 0, 8 * (4 + b) + k)
                        at = at_gla(4 + b, k)
                        mm = product(pe, ps[:, b, :], xc_hi[:, k, :], xc_lo[:, k, :], w_hi(at, BANK), w_lo(at, BANK),
                                     k, k == KT - 1)
                    if k1 == KT:
                        mm.then_inc(g_ready, 1)

                def lvl(n):
                    if not first or n >= 2:
                        pe.wait_ge(level_kept, of(c, NL + 1, n - 1))
                    if n == 0:
                        pe.wait_ge(q_scaled, c + 1)
                    else:
                        pe.wait_ge(z_done, of(c, NL, n))
                    for h in range(H):
                        z = zbuf[:, (n - 1) % 2, tile(h)]
                        mm = pe.matmul(ps[:, 4 + n % 2, tile(h)], qk[:, H + h, :] if n == 0 else z,
                                       qk[:, h, :] if n == 0 else z, start=True, stop=True)
                    mm.then_inc(level_ready, 1)

                lvl(0)
                gate(0, 0, KT)
                lvl(1)
                if not last:
                    gate_logits(c + 1)
                if not first:
                    turn_y(c - 1)
                lvl(2)
                gate(1, 0, KT // 2)
                lvl(3)
                lvl(4)
                gate(1, KT // 2, KT)
                if not last:
                    cumulate(c + 1)
                for n in range(5, NL + 1):
                    lvl(n)
                if not last:
                    pe.wait_ge(qk_decayed, of(c, 2, 2))
                    for h in range(H):
                        mm = pe.transpose(ps[:, 2, tile(h)], k_dec[:, h, :], ident[:, :])
                    mm.then_inc(k_turned, 1)
                if last:
                    pe.wait_ge(qk_decayed, 2 * c + 1)
                wait(pe, y_lo_done, of(c, 2, 0))
                wait(pe, state_done, of(c, H, 2))
                pe.wait_ge(level_kept, of(c, NL + 1, NL + 1))
                pe.wait_ge(v_ld, of(c, 16, 16))
                for h in range(H):
                    o = ps[:, 6 + h // 2, (h % 2) * DV:(h % 2 + 1) * DV]
                    pe.matmul(o, q_dec[:, h, :], state[:, h, :], start=True, stop=False)
                    mm = pe.matmul(o, att[:, h, :], v_sb[:, h * DV:(h + 1) * DV], start=False, stop=True)
                    if h % 2:
                        mm.then_inc(o_ready, 1)
                if not last:
                    pe.wait_ge(k_dec_t_done, c + 1)
                    pe.wait_ge(bcum_done, c + 2)
                    for h in range(H):
                        mm = pe.matmul(ps[:, 3 - h // 2, (h % 2) * DV:(h % 2 + 1) * DV], k_dec_t[:, h, :],
                                       v_sb[:, h * DV:(h + 1) * DV], start=True, stop=True)
                        if h % 2:
                            mm.then_inc(s_ready, 1)

            loop(pe, NC, chunk)
            for q in range(2 * TT):
                t, ch = q % TT, q // TT
                wait(pe, ao_added, q - 3)
                if ch == 0:
                    pe.wait_ge(y_moved, 32 * (t + 1))
                if q == 2:
                    pe.wait_ge(y_lo_done, 2 * NC)
                for k in range(KT):
                    if t == 0:
                        block_cut(pe, "gla", 0, 48 + 8 * ch + k)
                    at = at_gla(6 + ch, k)
                    mm = product(pe, ps[:, 4 + q % 4, :], x_hi[:, k, tile(t)], x_lo[:, k, tile(t)], w_hi(at, BANK),
                                 w_lo(at, BANK), k, k == KT - 1)
                mm.then_inc(ao_ready, 1)
                if q == 0:
                    turn_y(NC - 1)
                if ch and t >= 2:
                    norm_turn(pe, 1, t - 2, work[:, (t - 2) % 2, :])

            def ffn_pe(layer, n_in, n):
                s, name = fsem[layer], f"ffn{layer}"

                def step(i, last):
                    first = isinstance(i, int) and i == 0
                    for p in range(4):
                        hf, j = p // 2, p % 2
                        if first:
                            pe.wait_ge(x_lo_done[n_in], TT if p == 0 else 2 * TT)
                        wait(pe, s["silu_done"], of(i, 4, p - 1))
                        for which, bank in ((0, p % 2), (1, 2 + p % 2)):
                            if which:
                                wait(pe, s["prod_done"], of(i, 4, p - 1))
                            for k in range(KT):
                                if p == 0 and which == 0:
                                    block_cut(pe, name, i, k)
                                col = at_ffn(k) + which * FC + j * P
                                mm = product(pe, ps[:, bank, :], w_hi(col, P), w_lo(col, P), x_hi[:, k, half(hf)],
                                             x_lo[:, k, half(hf)], k, k == KT - 1)
                                if first and p == 0 and which == 0 and k == 3:
                                    norm_turn(pe, n_in, TT - 2, work[:, (TT - 2) % 2, :])
                            mm.then_inc(s["up_ready" if which else "gate_ready"], 1)
                            if first and p == 0 and which == 0:
                                norm_turn(pe, n_in, TT - 1, work[:, (TT - 1) % 2, :])
                    for t in range(TT):
                        if t % 4 == 0:
                            pe.wait_ge(s["h_lo_done"], of(i, 4, 2 + t // 2))
                        for ch in range(2):
                            q = 2 * t + ch
                            wait(pe, s["down_added"], of(i, 16, q - 3))
                            for k in range(FT):
                                if q == 0 or (q == 1):
                                    block_cut(pe, name, i, 8 + 2 * k + ch)
                                at = at_ffn(8 + 2 * k + ch)
                                mm = product(pe, ps[:, 4 + q % 4, :], h_hi[:, k, tile(t)], h_lo[:, k, tile(t)],
                                             w_hi(at, BANK), w_lo(at, BANK), k, k == FT - 1)
                            mm.then_inc(s["down_ready"], 1)
                        if last and n != 4 and t >= 2:
                            norm_turn(pe, n, t - 2, work[:, (t - 2) % 2, :])
                loop(pe, FSTEPS, step)

            ffn_pe(0, 1, 2)

            def gv(i, last):
                first = isinstance(i, int) and i == 0
                for par in range(2):
                    for t in range(TT):
                        if first and par == 0:
                            pe.wait_ge(x_lo_done[2], 2 * t + 2)
                        wait(pe, gv_biased, of(i, 16, 8 * par + t - 3))
                        for k in range(KT):
                            if t == 0:
                                block_cut(pe, "gv", i, 8 * par + k)
                            at = at_gv(8 * par + k)
                            mm = product(pe, ps[:, 4 + t % 4, 0:GC], x_hi[:, k, tile(t)], x_lo[:, k, tile(t)],
                                         w_hi(at, GC), w_lo(at, GC), k, k == KT - 1)
                        mm.then_inc(gv_ready, 1)
                        if first and par == 0 and t < 2:
                            norm_turn(pe, 2, TT - 2 + t, work[:, (TT - 2 + t) % 2, :])

            loop(pe, G // 2, gv)

            def gp(g, last):
                pe.wait_ge(ws_ld, of(g, 16, 16))
                wait(pe, gu_gelu, of(g, 6, 0))
                pe.transpose(ps[:, 1, 0:P], ws_raw[:, :], ident[:, :]).then_inc(ws_turned, 1)

                def spatial(q):
                    hf, e = q // 3, q % 3
                    if q == 0:
                        pe.wait_ge(ws_masked, g + 1)
                    pe.wait_ge(vn_done, of(g, TT, 4 * hf + 4))
                    wait(pe, sv_biased, of(g, 6, q - 1))
                    for c in range(4):
                        mm = pe.matmul(ps[:, 2 + q % 2, tile(c)], vn[:, 4 * hf + c, tile(e)], ws_t[:, :],
                                       start=True, stop=True)
                    mm.then_inc(sv_ready, 1)

                for q in range(6):
                    hf, e = q // 3, q % 3
                    wait(pe, gu_gelu, of(g, 6, q - 1))
                    if q == 1:
                        pe.wait_ge(ws_masked, g + 1)
                    for k in range(KT):
                        if q == 0:
                            block_cut(pe, "gp", g, k)
                        col = at_gp(k) + e * P
                        mm = product(pe, ps[:, q % 2, :], w_hi(col, P), w_lo(col, P), x_hi[:, k, half(hf)],
                                     x_lo[:, k, half(hf)], k, k == KT - 1)
                    mm.then_inc(gu_ready, 1)
                    if q >= 1:
                        spatial(q - 1)
                spatial(5)
                for t in range(TT):
                    if t % 4 == 0:
                        pe.wait_ge(m_lo_done, of(g, 6, 3 + 3 * (t // 4)))
                    for ch in range(2):
                        q = 2 * t + ch
                        wait(pe, go_added, of(g, 16, q - 3))
                        for k in range(GE):
                            if t == 0:
                                block_cut(pe, "gp", g, 8 + 2 * k + ch)
                            at = at_gp(8 + 2 * k + ch)
                            mm = product(pe, ps[:, 4 + q % 4, :], m_hi[:, k, tile(t)], m_lo[:, k, tile(t)],
                                         w_hi(at, BANK), w_lo(at, BANK), k, k == GE - 1)
                        mm.then_inc(go_ready, 1)
                    if last and t >= 2:
                        norm_turn(pe, 3, t - 2, work[:, (t - 2) % 2, :])

            loop(pe, G, gp)
            ffn_pe(1, 3, 4)


_INS = ["x", "norm_mix", "norm_ffn", "norm_final", "w_ffn_gate", "w_ffn_up", "w_ffn_down",
        "a_w_in", "a_w_gate2", "a_b_gate", "a_g_norm", "a_w_out",
        "b_w_in", "b_b_in", "b_ln_g", "b_ln_b", "b_w_s", "b_b_s", "b_w_out"]


def _constants():
    s, t = np.arange(P)[:, None], np.arange(P)[None, :]
    levels = [s == t] + [(s // (2 * b) == t // (2 * b)) & (s // b % 2 == 0) & (t // b % 2 == 1) for b in LEVELS]
    return {"level_masks": np.stack(levels, 1).astype(np.float32),
            "causal_matrix": (s <= t).astype(np.float32),
            "identity": np.eye(P, dtype=np.float32)}


def kernel(**inputs):
    import concourse.bacc as bacc
    from concourse.bass_utils import run_bass_kernel_spmd

    nc = bacc.Bacc("TRN2", target_bir_lowering=False, num_devices=1)
    arrays, args = {}, []
    given = {n: np.ascontiguousarray(inputs[n]) for n in _INS}
    given.update(_constants())
    for name, a in given.items():
        arrays[f"in_{name}"] = a
        args.append(nc.dram_tensor(f"in_{name}", a.shape, mybir.dt.from_np(a.dtype), kind="ExternalInput").ap())
    shape = given["x"].shape
    args.append(nc.dram_tensor("out_0", shape, F32, kind="ExternalOutput").ap())
    trunk_kernel(nc, *args)
    r = run_bass_kernel_spmd(nc, [arrays], core_ids=[0])
    return r.results[0]["out_0"]
```

```python
from contextlib import ExitStack

import numpy as np

import concourse.bass as bass
from concourse import mybir

F32 = mybir.dt.float32
FR = mybir.dt.float32r
U8 = mybir.dt.uint8
ALU = mybir.AluOpType
ACT = mybir.ActivationFunctionType

P = 128
EPS = 1e-6
BANK = 512
GLA_HEADS = 4
GLA_TAU = 16.0
STAGES = 4
LEVELS = [64, 32, 16, 8, 4, 2, 1]


class WeightBlocks:

    def __init__(self, phases):
        self.phase, self.slot, self.landed, self.before = {}, [], [], []
        value, last = [0] * STAGES, [0] * STAGES
        for name, iterations, dmas, slots in phases:
            self.phase[name] = (len(self.slot), len(dmas))
            for _ in range(iterations):
                for n_dmas, s in zip(dmas, slots):
                    self.before.append(last[s])
                    value[s] += 16 * n_dmas
                    self.slot.append(s)
                    self.landed.append(value[s])
                    last[s] = len(self.slot)

    def at(self, name, i, b):
        first, per = self.phase[name]
        if isinstance(i, int):
            n = first + per * i + b
            return self.slot[n], self.landed[n], n + 1, self.before[n]
        n = first + per + b
        step = self.landed[n + per] - self.landed[n]
        return (self.slot[n], (i - 1) * step + self.landed[n], (i - 1) * per + (n + 1),
                (i - 1) * per + self.before[n])


def trunk_kernel(nc, x, norm_mix, norm_ffn, norm_final, w_ffn_gate, w_ffn_up, w_ffn_down,
                 a_w_in, a_w_gate2, a_b_gate, a_g_norm, a_w_out,
                 b_w_in, b_b_in, b_ln_g, b_ln_b, b_w_s, b_b_s, b_w_out,
                 level_masks, causal_matrix, identity, out):
    _, S, D = x.shape
    F = w_ffn_gate.shape[2]
    KT = D // P
    TT = S // P
    HALVES = S // BANK
    H = GLA_HEADS
    DK, DV = D // (2 * H), D // H
    RANK = a_w_gate2.shape[1]
    o_k, o_v, o_g, o_a = H * DK, 2 * H * DK, 2 * H * DK + H * DV, 2 * H * DK + 2 * H * DV
    CH = P
    E = b_w_out.shape[1]
    G = b_w_s.shape[1]
    GC = E // G
    GE = GC // P
    VP = E // BANK
    FC = 256
    FT = FC // P
    FSTEPS = F // FC
    assert (KT, TT, HALVES, GE, FT) == (8, 8, 2, 3, 2) and F % FC == 0 and DK == P
    assert E % (2 * BANK) == 0 and 2 * RANK < P

    x_d = x.rearrange("b (t p) d -> (b t) p d", p=P)
    out_d = out.rearrange("b (t p) d -> (b t) p d", p=P)

    qk_d = nc.dram_tensor("qk_scratch", (2 * H, P, S), F32).ap()
    v_d = nc.dram_tensor("v_scratch", (S, D), F32).ap()
    al_d = nc.dram_tensor("a_lr_scratch", (2 * RANK, S), F32).ap()
    vv_d = nc.dram_tensor("gmlp_v_scratch", (TT, P, E), F32).ap()

    ring4 = [b % STAGES for b in range(12)]
    blocks = WeightBlocks([
        ("gla", 1, [1] * 64, ring4[:8] * 8),
        ("ffn0", FSTEPS, [2] * 8 + [1] * 4, ring4),
        ("gv", VP // 2, [1] * 16, ring4[:8] * 2),
        ("gp", G, [1] * 14, ring4 + [0, 1]),
        ("ffn1", FSTEPS, [2] * 8 + [1] * 4, ring4)])

    with ExitStack() as top:
        def make(stack, name, shape, dt=F32):
            return stack.enter_context(nc.sbuf_tensor(name, shape, dt))

        def sb(name, shape, dt=F32):
            return make(top, name, shape, dt)

        def sem(name):
            return top.enter_context(nc.semaphore(name))

        ps = top.enter_context(nc.psum_tensor("ps", [P, 8, BANK], F32))

        RING = 6144
        w_hi_main = sb("w_hi_main", [P, RING], FR)
        w_lo_main = sb("w_lo_main", [P, RING], FR)
        stage = sb("stage", [P, STAGES, BANK])
        x_hi = sb("x_hi", [P, KT, S], FR)
        x_lo = sb("x_lo", [P, KT, S], FR)
        ident = sb("ident", [P, P])
        gain_bc = sb("gain_bc", [P, D])
        eps_col = sb("eps_col", [P, 1])
        tick = sb("tick", [P, 1])
        causal = sb("causal", [P, P])
        stats = sb("stats", [P, 5, 3, TT])

        gla = ExitStack()

        def ga(name, shape, dt=F32):
            return make(gla, name, shape, dt)

        early = ExitStack()
        x_in = make(early, "x_in", [P, 2, D])
        xn0 = make(early, "xn0", [P, 2, D])
        x_more = make(early, "x_more", [P, 2, D])
        mask_stage = make(early, "mask_stage", [P, len(LEVELS) + 1, CH])
        al_sb = make(early, "al_sb", [2 * RANK, S])
        wa_stage = make(early, "wa_stage", [P, KT, RANK])
        wa_parts = make(early, "wa_parts", [P, KT, 2 * RANK], FR)
        evac = make(early, "evac", [P, 4, BANK])
        early.close()
        xc_hi = ga("xc_hi", [P, KT, CH], FR)
        xc_lo = ga("xc_lo", [P, KT, CH], FR)
        qk = ga("qk", [P, 2 * H, CH])
        al_c = ga("al_c", [2 * RANK + 1, CH])
        log_a = ga("log_a", [P, H * DK])
        bcum = ga("bcum", [P, H * CH])
        ebuf = ga("ebuf", [P, 2, H * CH])
        zbuf = ga("zbuf", [P, 2, H * CH])
        att = ga("att", [P, H, CH])
        q_dec = ga("q_dec", [P, H, CH])
        k_dec = ga("k_dec", [P, H, CH])
        k_dec_t = ga("k_dec_t", [P, H, CH])
        v_sb = ga("v_sb", [P, D])
        y_hi = ga("y_hi", [P, KT, CH], FR)
        y_lo = ga("y_lo", [P, KT, CH], FR)
        g_sb = ga("g_sb", [P, D])
        soft = ga("soft", [P, H * DK])
        state = ga("state", [P, H, DV])
        masks = ga("masks", [P, len(LEVELS) + 1, CH], U8)
        gnorm_bc = ga("gnorm_bc", [P, DV])
        w_gate2 = ga("w_gate2", [2 * RANK + 1, H * DK])
        eb_last = ga("eb_last", [P, H])
        ostat = ga("ostat", [P, 3, H])
        w_hi_more = ga("w_hi_more", [P, 8 * 2 * BANK - RING], FR)
        w_lo_more = ga("w_lo_more", [P, 8 * 2 * BANK - RING], FR)
        gla.close()

        resid = sb("resid", [P, TT, D])
        work = sb("work", [P, 2, D])
        ffn = ExitStack()
        h_hi = make(ffn, "h_hi", [P, FT, S], FR)
        h_lo = make(ffn, "h_lo", [P, FT, S], FR)
        prod = make(ffn, "prod", [P, 2, BANK])
        ffn.close()
        m_hi = sb("m_hi", [P, GE, S], FR)
        m_lo = sb("m_lo", [P, GE, S], FR)
        vn = sb("vn", [P, TT, GC])
        ln_g_bc = sb("ln_g_bc", [P, GC])
        ln_b_bc = sb("ln_b_bc", [P, GC])
        bs_bc = sb("bs_bc", [P, P])
        b_u = sb("b_u", [P, GE])
        ws_raw = sb("ws_raw", [P, P])
        ws_t = sb("ws_t", [P, P])
        st6 = sb("st6", [P, TT, 6])
        st_all = sb("st_all", [P, TT, VP, 6])
        mv = sb("mv", [P, TT, 2])
        dev = sb("dev", [P, TT])

        staged = [sem(f"staged_{s}") for s in range(STAGES)]
        w_hi_done, w_lo_done = sem("w_hi_done"), sem("w_lo_done")
        ident_ld, ones_ld = sem("ident_ld"), sem("ones_ld")
        const_ld, wa_ld, wa_hi_done, wa_lo_done, consts_set = (
            sem(n) for n in ("const_ld", "wa_ld", "wa_hi_done", "wa_lo_done", "consts_set"))
        gain_ld, masks_made = sem("gain_ld"), sem("masks_made")
        x_ld = [sem(f"x_ld_{s}") for s in range(4)]
        squared, rooted, inverted, normed = (
            [sem(f"{n}_{i}") for i in range(5)] for n in ("squared", "rooted", "inverted", "normed"))
        turned, x_hi_done, x_lo_done = (
            [sem(f"{n}_{i}") for i in range(4)] for n in ("turned", "x_hi_done", "x_lo_done"))
        al_ready, al_copied, al_stored = sem("al_ready"), sem("al_copied"), sem("al_stored")
        proj_ready, qk_copied, v_copied = sem("proj_ready"), sem("qk_copied"), sem("v_copied")
        evac_stored = [sem(f"evac_stored_{s}") for s in range(4)]
        al_ld, xc_ld, qk_ld, v_ld, y_moved = (sem(n) for n in ("al_ld", "xc_ld", "qk_ld", "v_ld", "y_moved"))
        z_ready, g_ready, cum_ready, y_turned, level_ready, k_turned, o_ready, s_ready = (
            sem(n) for n in ("z_ready", "g_ready", "cum_ready", "y_turned", "level_ready", "k_turned",
                             "o_ready", "s_ready"))
        z_abs, z_exp, z_soft, bcum_done, exp_done, q_exp, k_exp, last_exp, g_silu, k_dec_t_done, o_sq, o_root, \
            y_hi_done = (sem(n) for n in (
                "z_abs", "z_exp", "z_soft", "bcum_done", "exp_done", "q_exp", "k_exp", "last_exp", "g_silu",
                "k_dec_t_done", "o_sq", "o_root", "y_hi_done"))
        q_scaled, log_a_done, z_done, level_kept, qk_decayed, state_done, o_inv, y_done, y_lo_done = (
            sem(n) for n in ("q_scaled", "log_a_done", "z_done", "level_kept", "qk_decayed", "state_done",
                             "o_inv", "y_done", "y_lo_done"))
        exponent_done, g_gained = sem("exponent_done"), sem("g_gained")
        xr_ld = [sem(f"xr_ld_{s}") for s in range(2)]
        ao_ready, ao_added = sem("ao_ready"), sem("ao_added")
        f_names = ("gate_ready", "up_ready", "down_ready", "silu_done", "h_hi_done", "prod_done", "h_lo_done",
                   "down_added")
        fsem = [{n: sem(f"{n}_{layer}") for n in f_names} for layer in range(2)]
        bias_ld = [sem(f"bias_ld_{s}") for s in range(2)]
        gv_ready, gv_biased, gv_gelu, gv_stat, gv_kept, mv_done, dev_done, inv_done = (
            sem(n) for n in ("gv_ready", "gv_biased", "gv_gelu", "gv_stat", "gv_kept", "mv_done", "dev_done",
                             "inv_done"))
        gv_stored = [sem(f"gv_stored_{s}") for s in range(4)]
        ws_ld, bu_ld, ln_ld = (sem(n) for n in ("ws_ld", "bu_ld", "ln_ld"))
        vn_ld = [sem(f"vn_ld_{s}") for s in range(2)]
        ws_turned, ws_masked = sem("ws_turned"), sem("ws_masked")
        gu_ready, sv_ready, go_ready, gu_gelu, m_hi_done, sv_biased, m_done, m_lo_done, go_added = (
            sem(n) for n in ("gu_ready", "sv_ready", "go_ready", "gu_gelu", "m_hi_done", "sv_biased", "m_done",
                             "m_lo_done", "go_added"))
        vn_centred, vn_done = sem("vn_centred"), sem("vn_done")
        out_stored = [sem(f"out_stored_{s}") for s in range(5)]

        def wait(eng, s, value):
            if not isinstance(value, int) or value > 0:
                eng.wait_ge(s, value)

        def ring(main, more, at, n):
            return main[:, at:at + n] if at < RING else more[:, at - RING:at - RING + n]

        h_hi_flat = h_hi[:, :, :].rearrange("p j t -> p (j t)")
        h_lo_flat = h_lo[:, :, :].rearrange("p j t -> p (j t)")
        assert FT * S == 16 * BANK - RING

        def w_hi(at, n, more=None):
            return ring(w_hi_main, w_hi_more[:, :] if more is None else more, at, n)

        def w_lo(at, n, more=None):
            return ring(w_lo_main, w_lo_more[:, :] if more is None else more, at, n)

        def f32(ap):
            return ap.bitcast(F32)

        def k4(ap):
            return ap.rearrange("p (k t) -> p k t", k=4)

        def tile(t):
            return slice(t * P, (t + 1) * P)

        def half(h):
            return slice(h * BANK, (h + 1) * BANK)

        def of(i, per, k):
            return i * per + k

        def at_gla(m, k):
            return (m % 2) * 8 * BANK + k * BANK

        def at_ffn(b):
            return b * BANK

        def at_gv(b):
            return b * BANK

        def at_gp(b):
            return b * GC if b < 8 else 8 * GC + (b - 8) * BANK

        def src_gla(m, k):
            rows = slice(k * P, (k + 1) * P)
            col = [0, o_v, o_k, o_v + BANK, o_g, o_g + BANK][m] if m < 6 else (m - 6) * BANK
            return (a_w_in if m < 6 else a_w_out)[0, rows, col:col + BANK]

        def src_ffn(layer, i, b):
            if b < 8:
                cols = bass.ds(i * FC, FC)
                return [(0, FC, w_ffn_gate[layer, b * P:(b + 1) * P, cols]),
                        (FC, FC, w_ffn_up[layer, b * P:(b + 1) * P, cols])]
            kt, ch = (b - 8) // 2, (b - 8) % 2
            return [(0, BANK, w_ffn_down[layer, bass.ds(i * FC + kt * P, P), half(ch)])]

        def src_gv(i, b):
            panel = i * 2 + b // 8
            return [(0, BANK, b_w_in[0, (b % 8) * P:(b % 8 + 1) * P, bass.ds(panel * BANK + E, BANK)])]

        def src_gp(g, b):
            if b < 8:
                return [(0, GC, b_w_in[0, b * P:(b + 1) * P, bass.ds(g * GC, GC)])]
            kt, ch = (b - 8) // 2, (b - 8) % 2
            return [(0, BANK, b_w_out[0, bass.ds(g * GC + kt * P, P), half(ch)])]

        def src(name, i, b):
            if name == "gla":
                return [(0, BANK, src_gla(b // 8, b % 8))]
            if name == "gv":
                return src_gv(i, b)
            if name == "gp":
                return src_gp(i, b)
            return src_ffn(int(name[-1]), i, b)

        def place(name, b):
            if name == "gla":
                return at_gla(b // 8, b % 8), BANK
            if name == "gv":
                return at_gv(b), BANK
            if name == "gp":
                return at_gp(b), (GC if b < 8 else BANK)
            return at_ffn(b), BANK

        def load_block(sp, name, i, b):
            slot, _, _, before = blocks.at(name, i, b)
            wait(sp, w_lo_done, before)
            for col, n, source in src(name, i, b):
                sp.dma_start(stage[:, slot, col:col + n], source).then_inc(staged[slot], 16)

        def gla_used(m):
            if m < 4:
                return proj_ready, 8 * (m + 1)
            return (g_ready, 2 * NC - 5 + m) if m < 6 else (ao_ready, TT * (m - 5))

        def behind_level(first, last, n):
            if first and 1 <= n <= 4:
                return [40 + 2 * n - 2, 40 + 2 * n - 1]
            if last:
                return {1: [48], 2: [49], 3: [50], 4: [51], 5: [52], 6: [53, 54, 55]}.get(n, [])
            return []

        def cut_hi(act, name, i, b, used):
            slot, landed, _, _ = blocks.at(name, i, b)
            at, n = place(name, b)
            wait(act, staged[slot], landed)
            if used is not None:
                wait(act, used[0], used[1])
            more = h_hi_flat if name == "gv" else None
            nc.scalar.activation(w_hi(at, n, more), stage[:, slot, 0:n], ACT.Copy).then_inc(w_hi_done, 1)

        def cut_lo(pool, name, i, b):
            slot, _, count, _ = blocks.at(name, i, b)
            at, n = place(name, b)
            wait(pool, w_hi_done, count)
            hi, lo = (w_hi(at, n, h_hi_flat), w_lo(at, n, h_lo_flat)) if name == "gv" else (w_hi(at, n), w_lo(at, n))
            nc.gpsimd.tensor_tensor(lo, stage[:, slot, 0:n], f32(hi),
                                    ALU.subtract).then_inc(w_lo_done, 1)

        def block_cut(pe, name, i, b):
            wait(pe, w_lo_done, blocks.at(name, i, b)[2])

        def product(pe, bank, s_hi, s_lo, m_hi_, m_lo_, k, last):
            pe.matmul(bank, s_hi, m_hi_, start=(k == 0), stop=False)
            pe.matmul(bank, s_hi, m_lo_, start=False, stop=False)
            return pe.matmul(bank, s_lo, m_hi_, start=False, stop=last)

        def norm_square(act, n, t, source, slot):
            nc.scalar.activation(slot, source, ACT.Square,
                                 accum_out=stats[:, n, 0, t:t + 1]).then_inc(squared[n], 1)
            act.wait_ge(squared[n], t + 1)
            nc.scalar.activation(stats[:, n, 1, t:t + 1], stats[:, n, 0, t:t + 1], ACT.Sqrt,
                                 bias=eps_col[:, 0:1], scale=1.0 / D).then_inc(rooted[n], 1)

        def norm_apply(dve, n, t, source, slot):
            dve.wait_ge(rooted[n], t + 1)
            nc.vector.reciprocal(stats[:, n, 2, t:t + 1], stats[:, n, 1, t:t + 1]).then_inc(inverted[n], 1)
            dve.wait_ge(inverted[n], t + 1)
            dve.wait_ge(gain_ld, 16 * (n + 1))
            nc.vector.scalar_tensor_tensor(out=slot, in0=source, scalar=stats[:, n, 2, t:t + 1], in1=gain_bc[:, :],
                                           op0=ALU.mult, op1=ALU.mult).then_inc(normed[n], 1)

        def turn_bank(t, b):
            return 2 * b + (0 if t in (0, 2, 4) else 1)

        def norm_turn(pe, n, t, slot):
            pe.wait_ge(normed[n], t + 1)
            wait(pe, x_lo_done[n], 2 * (t - 1 if t < 6 else t))
            for k in range(KT):
                mm = pe.transpose(ps[:, turn_bank(t, k // 4), tile(k % 4)], slot[:, tile(k)], ident[:, :])
                if k % 4 == 3:
                    mm.then_inc(turned[n], 1)

        def norm_hi(act, n, t):
            for b in range(2):
                act.wait_ge(turned[n], 2 * t + b + 1)
                nc.scalar.activation(x_hi[:, 4 * b:4 * b + 4, tile(t)], k4(ps[:, turn_bank(t, b), :]),
                                     ACT.Copy).then_inc(x_hi_done[n], 1)

        def norm_lo(dve, n, t):
            for b in range(2):
                dve.wait_ge(x_hi_done[n], 2 * t + b + 1)
                nc.vector.tensor_tensor(x_lo[:, 4 * b:4 * b + 4, tile(t)], k4(ps[:, turn_bank(t, b), :]),
                                        f32(x_hi[:, 4 * b:4 * b + 4, tile(t)]),
                                        ALU.subtract).then_inc(x_lo_done[n], 1)

        def x_slot(t):
            return (x_in if t % 4 < 2 else x_more)[:, t % 2, :]

        vn_flat = vn[:, :, :].rearrange("p t c -> p (t c)")

        vb = vn_flat[:, 0:2 * BANK].rearrange("p (s c) -> p s c", s=2)
        vg = vn_flat[:, 2 * BANK:6 * BANK].rearrange("p (s c) -> p s c", s=4)
        v_bias = prod[:, :, :]

        def out_slot(t):
            s = t % 5
            return work[:, s, :] if s < 2 else vn_flat[:, (s - 2) * D:(s - 1) * D]

        def level(ap, b):
            return ap.rearrange("p (m two b) -> p m two b", two=2, b=b)

        qk_flat = qk[:, :, :].rearrange("p h t -> p (h t)")
        q_all, k_all = qk_flat[:, 0:H * CH], qk_flat[:, H * CH:2 * H * CH]
        NL = len(LEVELS)
        NC = S // CH
        HC = CH // 2
        assert LEVELS[0] == HC

        def loop(eng, n, body):
            body(0, False)
            with eng.Fori(1, n - 1) as i:
                body(i, False)
            body(n - 1, True)

        block = top.enter_context(nc.Block())

        @block.sync
        def _(sp):
            def load_x(t):
                wait(sp, normed[0], t - 3)
                sp.dma_start(x_slot(t), x_d[t]).then_inc(x_ld[t % 4], 16)

            load_x(0)
            sp.dma_start(gain_bc[:, :], norm_mix[0].partition_broadcast(P)).then_inc(gain_ld, 16)
            load_x(1)
            sp.dma_start(ident[:, :], identity).then_inc(ident_ld, 16)
            load_x(2)
            load_block(sp, "gla", 0, 0)
            load_block(sp, "gla", 0, 1)
            load_x(3)
            for b in range(2, 5):
                load_block(sp, "gla", 0, b)
            load_x(4)
            for b in range(5, 8):
                load_block(sp, "gla", 0, b)
            for t in range(5, TT):
                load_x(t)
            sp.dma_start(wa_stage[:, :, :], a_w_in[0, :, o_a:o_a + RANK].rearrange("(k p) r -> p k r", p=P)
                         ).then_inc(wa_ld, 16)
            sp.dma_start(mask_stage[:, :, :], level_masks).then_inc(const_ld, 16)
            sp.dma_start(causal[:, :], causal_matrix).then_inc(const_ld, 16)
            sp.dma_start(gnorm_bc[:, :], a_g_norm[0].partition_broadcast(P)).then_inc(const_ld, 16)
            for r in (0, RANK):
                sp.dma_start(w_gate2[r:r + RANK, :], a_w_gate2[0]).then_inc(const_ld, 16)
            sp.dma_start(w_gate2[2 * RANK:2 * RANK + 1, :], a_b_gate).then_inc(const_ld, 16)

            def chunk_loads(col, which):
                cols = bass.ds(col, CH)
                if which == "al":
                    sp.dma_start(al_c[0:2 * RANK, :], al_d[:, cols]).then_inc(al_ld, 16)
                elif which == "xc":
                    sp.dma_start(f32(xc_hi[:, :, :]), f32(x_hi[:, :, cols])).then_inc(xc_ld, 16)
                    sp.dma_start(f32(xc_lo[:, :, :]), f32(x_lo[:, :, cols])).then_inc(xc_ld, 16)
                elif which == "qk":
                    sp.dma_start(qk[:, :, :], qk_d[:, :, cols].rearrange("h p t -> p h t")).then_inc(qk_ld, 16)
                else:
                    sp.dma_start(v_sb[:, :], v_d[cols, :]).then_inc(v_ld, 16)

            for m in range(4):
                if m == 2:
                    sp.wait_ge(al_copied, HALVES)
                    sp.dma_start(al_d, al_sb[:, :]).then_inc(al_stored, 16)
                if m == 3:
                    sp.wait_ge(turned[0], 2 * TT)
                    sp.wait_ge(x_lo_done[0], 2 * TT)
                    sp.wait_ge(al_stored, 16)
                    sp.dma_start(al_c[2 * RANK:2 * RANK + 1, :], causal_matrix[0:1, :]).then_inc(ones_ld, 16)
                    chunk_loads(0, "al")
                    chunk_loads(0, "xc")
                for j in range(8):
                    if j < 4:
                        load_block(sp, "gla", 0, 8 * (m + 1) + 2 * j)
                        load_block(sp, "gla", 0, 8 * (m + 1) + 2 * j + 1)
                    q = 8 * m + j
                    if m % 2 == 0:
                        sp.wait_ge(qk_copied, 8 * (m // 2) + j + 1)
                        dst = qk_d[(m // 2) * H + j % H, :, half(j // H)]
                    else:
                        sp.wait_ge(v_copied, 8 * (m // 2) + j + 1)
                        dst = v_d[tile(j), half(m // 2)]
                    sp.dma_start(dst, evac[:, q % 4, :]).then_inc(evac_stored[q % 4], 16)
                    if q == 25:
                        for s in range(4):
                            sp.wait_ge(evac_stored[s], 16 * 6)
                        chunk_loads(0, "qk")
            for b in range(40, 44):
                load_block(sp, "gla", 0, b)
            for s in range(4):
                sp.wait_ge(evac_stored[s], 16 * 8)
            chunk_loads(0, "v")
            sp.wait_ge(z_ready, 1)
            chunk_loads(CH, "al")
            for b in range(44, 48):
                load_block(sp, "gla", 0, b)

            def at(value):
                return value if isinstance(value, int) else sp.snap(value)

            def move_y(c, col):
                sp.wait_ge(y_lo_done, of(c, 2, 2))
                cols = bass.ds(col, CH)
                sp.dma_start(f32(x_hi[:, :, cols]), f32(y_hi[:, :, :])).then_inc(y_moved, 16)
                sp.dma_start(f32(x_lo[:, :, cols]), f32(y_lo[:, :, :])).then_inc(y_moved, 16)

            def chunk(c, last):
                before, after = at((c - 1) * CH), at((c + 1) * CH)
                if not isinstance(c, int) or c > 0:
                    move_y(c - 1, before)
                if not last:
                    sp.wait_ge(g_ready, of(c, 2, 2))
                    if not isinstance(c, int) or c < NC - 2:
                        chunk_loads((c + 2) * CH, "al")
                    chunk_loads(after, "xc")
                    sp.wait_ge(qk_decayed, of(c, 2, 2))
                    sp.wait_ge(z_done, of(c, NL, NL))
                    sp.wait_ge(level_ready, of(c, NL + 1, 1))
                    chunk_loads(after, "qk")
                    sp.wait_ge(s_ready, of(c, 2, 2))
                    chunk_loads(after, "v")

            def residual(t):
                sp.dma_start(resid[:, t, :], x_d[t]).then_inc(xr_ld[t // 3 > 0], 16)

            chunk(0, False)
            with sp.Fori(1, NC - 2) as c:
                chunk(c, False)
            chunk(NC - 2, False)
            for b in range(48, 52):
                load_block(sp, "gla", 0, b)
            chunk(NC - 1, True)
            for b in range(52, 56):
                load_block(sp, "gla", 0, b)
            sp.wait_ge(g_ready, 2 * NC)
            residual(0)
            residual(1)
            sp.wait_ge(qk_decayed, 2 * NC - 1)
            sp.wait_ge(z_done, NL * NC)
            sp.wait_ge(level_ready, (NL + 1) * (NC - 1) + 1)
            residual(2)
            sp.wait_ge(o_ready, 2 * NC)
            for t in range(3, TT):
                residual(t)
            for b in range(56, 60):
                load_block(sp, "gla", 0, b)
            move_y(NC - 1, (NC - 1) * CH)
            for b in range(60, 64):
                load_block(sp, "gla", 0, b)
            sp.wait_ge(normed[0], TT)
            sp.dma_start(gain_bc[:, :], norm_ffn[0].partition_broadcast(P)).then_inc(gain_ld, 16)
            for b in range(8):
                load_block(sp, "ffn0", 0, b)

            def ffn_loads(layer):
                name = f"ffn{layer}"

                def step(i, last):
                    for b in range(8, 12):
                        load_block(sp, name, i, b)
                    if not last:
                        for b in range(8):
                            load_block(sp, name, i + 1, b)
                loop(sp, FSTEPS, step)

            sp.wait_ge(normed[1], TT)
            sp.dma_start(gain_bc[:, :], norm_mix[1].partition_broadcast(P)).then_inc(gain_ld, 16)
            ffn_loads(0)
            for b in range(8):
                load_block(sp, "gv", 0, b)
            for s in range(2):
                sp.wait_ge(fsem[0]["down_ready"], 16 * FSTEPS)
                sp.dma_start(v_bias[:, s, :], b_b_in[0, E + s * BANK:E + (s + 1) * BANK].partition_broadcast(P)
                             ).then_inc(bias_ld[s], 16)

            def gv(i, last):
                for par in range(2):
                    for j in range(4):
                        if par == 0:
                            load_block(sp, "gv", i, 8 + 2 * j)
                            load_block(sp, "gv", i, 8 + 2 * j + 1)
                        elif not last:
                            load_block(sp, "gv", i + 1, 2 * j)
                            load_block(sp, "gv", i + 1, 2 * j + 1)
                        else:
                            load_block(sp, "gp", 0, 2 * j)
                            load_block(sp, "gp", 0, 2 * j + 1)
                        for t in (2 * j, 2 * j + 1):
                            sp.wait_ge(gv_gelu, of(i, 16, 8 * par + t + 1))
                            sp.dma_start(vv_d[t, :, bass.ds(i * (2 * BANK) + par * BANK, BANK)],
                                         vg[:, t % 4, :]).then_inc(gv_stored[t % 4], 16)
                    if not last:
                        sp.wait_ge(gv_biased, of(i, 16, 8 * par + 8))
                        sp.dma_start(v_bias[:, par, :],
                                     b_b_in[0, bass.ds((i + 1) * (2 * BANK) + (E + par * BANK), BANK)
                                            ].partition_broadcast(P)
                                     ).then_inc(bias_ld[par], 16)

            def group_loads(g):
                small_loads(g)
                v_loads(g)
                norm_loads(g)

            def small_loads(g):
                sp.dma_start(ws_raw[:, :], b_w_s[0, bass.ds(g, 1)].rearrange("g t s -> t (g s)")).then_inc(ws_ld, 16)
                sp.dma_start(b_u[:, :], b_b_in[0, bass.ds(g * GC, GC)].rearrange("(e p) -> p e", p=P),
                             allow_slow_non_contiguous=True).then_inc(bu_ld, 16)
                sp.dma_start(bs_bc[:, :], b_b_s[0, bass.ds(g, 1)].rearrange("g t -> (g t)").partition_broadcast(P)
                             ).then_inc(bu_ld, 16)

            def v_loads(g):
                for t in range(TT):
                    sp.dma_start(vn[:, t, :], vv_d[t, :, bass.ds(g * GC, GC)]).then_inc(vn_ld[t // 4], 16)

            def norm_loads(g):
                wait(sp, vn_done, of(g, TT, 0))
                cols = bass.ds(g * GC, GC)
                sp.dma_start(ln_g_bc[:, :], b_ln_g[0, cols].partition_broadcast(P)).then_inc(ln_ld, 16)
                sp.dma_start(ln_b_bc[:, :], b_ln_b[0, cols].partition_broadcast(P)).then_inc(ln_ld, 16)

            small_loads(0)
            norm_loads(0)
            loop(sp, VP // 2, gv)
            for s in range(4):
                sp.wait_ge(gv_stored[s], 16 * VP * TT // 4)
            sp.wait_ge(gv_stat, TT * VP)
            v_loads(0)
            sp.wait_ge(normed[2], TT)
            sp.dma_start(gain_bc[:, :], norm_ffn[1].partition_broadcast(P)).then_inc(gain_ld, 16)

            def gp(g, last):
                for b in range(8, 14):
                    load_block(sp, "gp", g, b)
                if not last:
                    sp.wait_ge(sv_ready, of(g, 6, 6))
                    sp.wait_ge(gu_gelu, of(g, 6, 6))
                    sp.wait_ge(sv_biased, of(g, 6, 6))
                    group_loads(g + 1)
                    for b in range(8):
                        load_block(sp, "gp", g + 1, b)
                else:
                    for b in range(8):
                        load_block(sp, "ffn1", 0, b)

            loop(sp, G, gp)
            sp.wait_ge(normed[3], TT)
            sp.dma_start(gain_bc[:, :], norm_final.partition_broadcast(P)).then_inc(gain_ld, 16)
            ffn_loads(1)
            for t in range(TT):
                sp.wait_ge(normed[4], t + 1)
                sp.dma_start(out_d[t], out_slot(t)).then_inc(out_stored[t % 5], 16)
            for s in range(5):
                sp.wait_ge(out_stored[s], 16 * ((TT - 1 - s) // 5 + 1))

        @block.gpsimd
        def _(pool):
            nc.gpsimd.memset(eps_col[:, :], EPS).then_inc(consts_set, 1)
            for b in range(8):
                cut_lo(pool, "gla", 0, b)
            pool.wait_ge(wa_hi_done, 1)
            nc.gpsimd.tensor_tensor(wa_parts[:, :, RANK:], wa_stage[:, :, :], f32(wa_parts[:, :, 0:RANK]),
                                    ALU.subtract).then_inc(wa_lo_done, 1)
            for b in range(8, 40):
                cut_lo(pool, "gla", 0, b)

            def chunk(c, last):
                pool.wait_ge(bcum_done, c + 1)
                for n, b in enumerate(LEVELS):
                    bv, ev = level(bcum[:, :], b), level(ebuf[:, n % 2, :], b)
                    edge = bv[:, :, 0, b - 1:b].to_broadcast([P, H * CH // (2 * b), b])
                    wait(pool, z_done, of(c, NL, max(n - 1, 0)))
                    nc.gpsimd.tensor_tensor(ev[:, :, 1, :], bv[:, :, 1, :], edge, ALU.subtract)
                    nc.gpsimd.tensor_tensor(ev[:, :, 0, :], edge, bv[:, :, 0, :],
                                            ALU.subtract).then_inc(exponent_done, 1)
                    for b8 in behind_level(isinstance(c, int) and c == 0, last, n - 1):
                        cut_lo(pool, "gla", 0, b8)
                for b8 in behind_level(isinstance(c, int) and c == 0, last, NL - 1):
                    cut_lo(pool, "gla", 0, b8)
                pool.wait_ge(g_silu, of(c, 2, 2))
                gv_ = g_sb[:, :].rearrange("p (h e) -> p h e", h=H)
                for h in range(H):
                    gain = nc.gpsimd.tensor_tensor(gv_[:, h, :], gv_[:, h, :], gnorm_bc[:, :], ALU.mult)
                gain.then_inc(g_gained, 1)
                if last:
                    for b in range(56, 64):
                        cut_lo(pool, "gla", 0, b)

            pool.wait_ge(const_ld, 16 * 6)
            loop(pool, NC, chunk)
            for b in range(8):
                cut_lo(pool, "ffn0", 0, b)

            def ffn_cuts(layer, after):
                name = f"ffn{layer}"

                def step(i, last):
                    for b in range(8, 12):
                        cut_lo(pool, name, i, b)
                    for b in range(8):
                        if not last:
                            cut_lo(pool, name, i + 1, b)
                        elif after:
                            cut_lo(pool, after, 0, b)
                loop(pool, FSTEPS, step)

            ffn_cuts(0, "gv")

            def gv(i, last):
                for b in range(8, 16):
                    cut_lo(pool, "gv", i, b)
                for b in range(8):
                    if not last:
                        cut_lo(pool, "gv", i + 1, b)
                    else:
                        cut_lo(pool, "gp", 0, b)

            loop(pool, VP // 2, gv)

            def gp(g, last):
                for b in range(8, 14):
                    cut_lo(pool, "gp", g, b)
                for b in range(8):
                    if not last:
                        cut_lo(pool, "gp", g + 1, b)
                    else:
                        cut_lo(pool, "ffn1", 0, b)

            loop(pool, G, gp)
            ffn_cuts(1, None)

        @block.scalar
        def _(act):
            act.wait_ge(consts_set, 1)
            nc.scalar.activation(tick[:, :], eps_col[:, :], ACT.Sqrt)
            for t in range(TT):
                act.wait_ge(x_ld[t % 4], 16 * (t // 4 + 1))
                wait(act, turned[0], 2 * (t - 1))
                norm_square(act, 0, t, x_slot(t), xn0[:, t % 2, :])
                if t >= 1:
                    norm_hi(act, 0, t - 1)
                if 1 <= t <= 4:
                    cut_hi(act, "gla", 0, 2 * t - 2, None)
                    cut_hi(act, "gla", 0, 2 * t - 1, None)
            norm_hi(act, 0, TT - 1)
            act.wait_ge(wa_ld, 16)
            nc.scalar.activation(wa_parts[:, :, 0:RANK], wa_stage[:, :, :], ACT.Copy).then_inc(wa_hi_done, 1)

            def exp_abs(c):
                act.wait_ge(z_ready, c + 1)
                wait(act, log_a_done, of(c, 1, 0))
                nc.scalar.activation(soft[:, :], ps[:, 2, :], ACT.Abs).then_inc(z_abs, 1)
                act.wait_ge(z_abs, c + 1)
                nc.scalar.activation(soft[:, :], soft[:, :], ACT.Exp, scale=-1.0).then_inc(z_exp, 1)

            def softplus(c):
                act.wait_ge(z_exp, c + 1)
                nc.scalar.activation(soft[:, :], soft[:, :], ACT.Ln, bias=1.0).then_inc(z_soft, 1)

            for m in range(4):
                for j in range(8):
                    if j < 4:
                        cut_hi(act, "gla", 0, 8 * (m + 1) + 2 * j, gla_used(m - 1) if m else None)
                        cut_hi(act, "gla", 0, 8 * (m + 1) + 2 * j + 1, gla_used(m - 1) if m else None)
                    if m % 2 == 0:
                        q = 8 * m + j
                        act.wait_ge(proj_ready, q + 1)
                        wait(act, evac_stored[q % 4], 16 * (q // 4))
                        nc.scalar.activation(evac[:, q % 4, :], ps[:, 4 + q % 4, :], ACT.Copy).then_inc(qk_copied, 1)
                    if m == 1 and j == 0:
                        for h in range(HALVES):
                            act.wait_ge(al_ready, h + 1)
                            nc.scalar.activation(al_sb[:, half(h)], ps[0:2 * RANK, 2 * h, :], ACT.Copy
                                                 ).then_inc(al_copied, 1)
            act.wait_ge(al_ld, 16)
            exp_abs(0)
            softplus(0)
            def turn_hi(c):
                wait(act, y_moved, of(c, 32, 0))
                for b in range(2):
                    act.wait_ge(y_turned, of(c, 2, b + 1))
                    nc.scalar.activation(y_hi[:, 4 * b:4 * b + 4, :], k4(ps[:, 6 + b, :]), ACT.Copy
                                         ).then_inc(y_hi_done, 1)

            def cumulated(c):
                act.wait_ge(cum_ready, c + 1)
                wait(act, exponent_done, of(c, NL, 0))
                wait(act, last_exp, of(c, 1, 0))
                nc.scalar.activation(bcum[:, :], ps[:, 3, :], ACT.Copy, scale=1.0 / GLA_TAU).then_inc(bcum_done, 1)

            def chunk(c, last):
                first = isinstance(c, int) and c == 0

                def expo(n):
                    act.wait_ge(exponent_done, of(c, NL, n + 1))
                    nc.scalar.activation(ebuf[:, n % 2, :], ebuf[:, n % 2, :], ACT.Exp).then_inc(exp_done, 1)

                def panel_part(n):
                    for b in behind_level(first, last, n):
                        cut_hi(act, "gla", 0, b, gla_used(3 if first else 4))

                expo(0)
                expo(1)
                panel_part(1)
                act.wait_ge(bcum_done, c + 1)
                wait(act, o_ready, of(c, 2, 0))
                nc.scalar.activation(q_dec[:, :, :], bcum[:, :].rearrange("p (h t) -> p h t", h=H), ACT.Exp
                                     ).then_inc(q_exp, 1)
                if not last:
                    exp_abs(c + 1)
                expo(2)
                panel_part(2)
                if not first:
                    turn_hi(c - 1)
                expo(3)
                panel_part(3)
                if not last:
                    softplus(c + 1)
                expo(4)
                panel_part(4)
                if not last:
                    wait(act, k_turned, of(c, 1, 0))
                    for h in range(H):
                        nc.scalar.activation(k_dec[:, h, :], bcum[:, tile(h)], ACT.Exp, scale=-1.0,
                                             bias=bcum[:, h * CH + CH - 1:h * CH + CH]).then_inc(k_exp, 1)
                    wait(act, state_done, of(c, H, 2))
                    nc.scalar.activation(eb_last[:, :], bcum[:, CH - 1::CH], ACT.Exp).then_inc(last_exp, 1)
                expo(5)
                panel_part(5)
                expo(6)
                panel_part(6)
                if not last:
                    cumulated(c + 1)
                wait(act, y_turned, of(c, 2, 0))
                for b in range(2):
                    act.wait_ge(g_ready, of(c, 2, b + 1))
                    nc.scalar.activation(g_sb[:, half(b)], ps[:, b, :], ACT.Silu).then_inc(g_silu, 1)
                if not last:
                    act.wait_ge(k_turned, c + 1)
                    wait(act, s_ready, of(c, 2, 0))
                    nc.scalar.activation(k_dec_t[:, :, :], k4(ps[:, 2, :]), ACT.Copy).then_inc(k_dec_t_done, 1)
                    act.wait_ge(log_a_done, c + 2)
                for h in range(H):
                    act.wait_ge(o_ready, of(c, 2, h // 2 + 1))
                    nc.scalar.activation(soft[:, 0:DV], ps[:, 6 + h // 2, (h % 2) * DV:(h % 2 + 1) * DV],
                                         ACT.Square, accum_out=ostat[:, 0, h:h + 1]).then_inc(o_sq, 1)
                    act.wait_ge(o_sq, of(c, H, h + 1))
                nc.scalar.activation(ostat[:, 1, :], ostat[:, 0, :], ACT.Sqrt, bias=eps_col[:, 0:1],
                                     scale=1.0 / DV).then_inc(o_root, 1)

            cumulated(0)
            loop(act, NC, chunk)
            turn_hi(NC - 1)
            for b in range(56, 64):
                cut_hi(act, "gla", 0, b, gla_used(5))
            for t in range(TT + 2):
                if t < TT:
                    act.wait_ge(ao_added, TT + t + 1)
                    wait(act, turned[1], 2 * (t - 1))
                    norm_square(act, 1, t, resid[:, t, :], work[:, t % 2, :])
                    if t < 4:
                        cut_hi(act, "ffn0", 0, 2 * t, gla_used(6))
                        cut_hi(act, "ffn0", 0, 2 * t + 1, gla_used(6))
                if t >= 2:
                    norm_hi(act, 1, t - 2)

            def ffn_act(layer, n, after):
                s, name = fsem[layer], f"ffn{layer}"
                before = (go_ready, 16 * G) if layer else gla_used(7)

                def step(i, last):
                    for p in range(4):
                        hf, j = p // 2, p % 2
                        act.wait_ge(s["gate_ready"], of(i, 4, p + 1))
                        wait(act, s["prod_done"], of(i, 4, p - 1))
                        nc.scalar.activation(work[:, 0, half(p % 2)], ps[:, p % 2, :], ACT.Silu
                                             ).then_inc(s["silu_done"], 1)
                        cut_hi(act, name, i, 8 + p,
                               before if isinstance(i, int) and i == 0 else (s["down_ready"], of(i, 16, 0)))
                        act.wait_ge(s["prod_done"], of(i, 4, p + 1))
                        nc.scalar.activation(h_hi[:, j, half(hf)], prod[:, p % 2, :], ACT.Copy
                                             ).then_inc(s["h_hi_done"], 1)
                    if not last:
                        for b in range(8):
                            cut_hi(act, name, i + 1, b, (s["up_ready"], of(i, 4, 4)))
                        return
                    for t in range(TT + (2 if after else 0)):
                        if t < TT:
                            act.wait_ge(s["down_added"], 16 * i + 2 * t + 2)
                            if after:
                                wait(act, turned[n], 2 * (t - 1))
                                if t < 4:
                                    cut_hi(act, after, 0, 2 * t, (s["up_ready"], of(i, 4, 4)))
                                    cut_hi(act, after, 0, 2 * t + 1, (s["up_ready"], of(i, 4, 4)))
                            else:
                                wait(act, out_stored[t % 5], 16 * (t // 5))
                            norm_square(act, n, t, resid[:, t, :], work[:, t % 2, :] if after else out_slot(t))
                        if after and t >= 2:
                            norm_hi(act, n, t - 2)
                loop(act, FSTEPS, step)

            ffn_act(0, 2, "gv")

            def gv(i, last):
                for par in range(2):
                    for t in range(TT):
                        act.wait_ge(gv_biased, of(i, 16, 8 * par + t + 1))
                        wait(act, gv_stat, of(i, 16, 8 * par + t - 3))
                        q4 = 2 * par + t // 4
                        wait(act, gv_stored[t % 4], of(i, 64, 16 * q4))
                        nc.scalar.activation(vg[:, t % 4, :], vb[:, t % 2, :], ACT.Gelu_apprx_tanh
                                             ).then_inc(gv_gelu, 1)
                        free = (gv_ready, of(i, 16, 8 * par))
                        if par == 0 and isinstance(i, int) and i == 0:
                            free = (fsem[0]["down_ready"], 16 * FSTEPS)
                        if par == 0:
                            cut_hi(act, "gv", i, 8 + t, free)
                        elif not last:
                            cut_hi(act, "gv", i + 1, t, free)
                        else:
                            cut_hi(act, "gp", 0, t, free)

            loop(act, VP // 2, gv)
            act.wait_ge(mv_done, TT)
            nc.scalar.activation(dev[:, :], mv[:, :, 1], ACT.Sqrt, bias=eps_col[:, 0:1]).then_inc(dev_done, 1)

            def gp(g, last):
                outputs_used = (go_ready, of(g, 16, 0)) if not isinstance(g, int) or g else (gv_ready, TT * VP)
                act.wait_ge(bu_ld, of(g, 32, 32))
                for q in range(6):
                    hf, e = q // 3, q % 3
                    act.wait_ge(gu_ready, of(g, 6, q + 1))
                    wait(act, m_done, of(g, 6, q - 1))
                    nc.scalar.activation(work[:, 0, half(q % 2)], ps[:, q % 2, :], ACT.Gelu_apprx_tanh,
                                         bias=b_u[:, e:e + 1]).then_inc(gu_gelu, 1)
                    for b in [(8, 9), (10, 11), (12,), (13,), (), ()][q]:
                        cut_hi(act, "gp", g, b, outputs_used)
                    act.wait_ge(m_done, of(g, 6, q + 1))
                    nc.scalar.activation(m_hi[:, e, half(hf)], work[:, 1, half(q % 2)], ACT.Copy
                                         ).then_inc(m_hi_done, 1)
                if not last:
                    for b in range(8):
                        cut_hi(act, "gp", g + 1, b, (gu_ready, of(g, 6, 6)))
                    return
                for t in range(TT + 2):
                    if t < TT:
                        act.wait_ge(go_added, 16 * g + 2 * t + 2)
                        wait(act, turned[3], 2 * (t - 1))
                        norm_square(act, 3, t, resid[:, t, :], work[:, t % 2, :])
                        if t < 3:
                            cut_hi(act, "ffn1", 0, 2 * t, (gu_ready, 6 * G))
                            cut_hi(act, "ffn1", 0, 2 * t + 1, (gu_ready, 6 * G))
                    if t == TT:
                        cut_hi(act, "ffn1", 0, 6, (go_ready, 16 * G))
                        cut_hi(act, "ffn1", 0, 7, (go_ready, 16 * G))
                    if t >= 2:
                        norm_hi(act, 3, t - 2)

            loop(act, G, gp)
            ffn_act(1, 4, None)

        @block.vector
        def _(dve):
            for t in range(TT):
                norm_apply(dve, 0, t, x_slot(t), xn0[:, t % 2, :])
                if t >= 1:
                    norm_lo(dve, 0, t - 1)
            norm_lo(dve, 0, TT - 1)
            dve.wait_ge(const_ld, 16 * 6)
            nc.vector.tensor_copy(masks[:, :, :], mask_stage[:, :, :]).then_inc(masks_made, 1)

            dve.wait_ge(masks_made, 1)
            nc.vector.memset(state[:, :, :], 0.0).then_inc(state_done, 1)
            nc.vector.memset(att[:, :, :], 0.0).then_inc(state_done, 1)

            def log_sigmoid(c):
                dve.wait_ge(z_soft, c + 1)
                wait(dve, cum_ready, of(c, 1, 0))
                nc.vector.scalar_tensor_tensor(out=log_a[:, :], in0=ps[:, 2, :], scalar=0.0, in1=soft[:, :],
                                               op0=ALU.min, op1=ALU.subtract).then_inc(log_a_done, 1)

            def scale_q(c):
                dve.wait_ge(qk_ld, of(c, 16, 16))
                nc.vector.tensor_scalar(q_all, q_all, float(DK) ** -0.5, None, ALU.mult).then_inc(q_scaled, 1)

            for m in (1, 3):
                for j in range(8):
                    q = 8 * m + j
                    dve.wait_ge(proj_ready, q + 1)
                    dve.wait_ge(evac_stored[q % 4], 16 * (q // 4))
                    nc.vector.tensor_copy(evac[:, q % 4, :], ps[:, 4 + q % 4, :]).then_inc(v_copied, 1)
                    if m == 3 and j == 4:
                        dve.wait_ge(al_ld, 16)
                        log_sigmoid(0)
                    if m == 3 and j == 6:
                        scale_q(0)
            dve.wait_ge(state_done, 2)

            def turn_lo(c):
                for b in range(2):
                    dve.wait_ge(y_hi_done, of(c, 2, b + 1))
                    nc.vector.tensor_tensor(y_lo[:, 4 * b:4 * b + 4, :], k4(ps[:, 6 + b, :]),
                                            f32(y_hi[:, 4 * b:4 * b + 4, :]), ALU.subtract).then_inc(y_lo_done, 1)

            def chunk(c, last):
                first = isinstance(c, int) and c == 0
                dve.wait_ge(q_scaled, c + 1)

                def keep(n):
                    dve.wait_ge(level_ready, of(c, NL + 1, n + 1))
                    if n == 0:
                        wait(dve, o_ready, of(c, 2, 0))
                    else:
                        dve.wait_ge(level_kept, of(c, NL + 1, n))
                    if n == 1:
                        nc.vector.tensor_copy(att[0:HC, :, HC:CH], k4(ps[:, 5, :])[0:HC, :, HC:CH]
                                              ).then_inc(level_kept, 1)
                        return
                    nc.vector.tensor_copy(tick[:, :], eps_col[:, :])
                    nc.vector.copy_predicated(att[:, :, :], masks[:, n:n + 1, :].to_broadcast([P, H, CH]),
                                              k4(ps[:, 4 + n % 2, :])).then_inc(level_kept, 1)

                for n, b in enumerate(LEVELS):
                    dve.wait_ge(exp_done, of(c, NL, n + 1))
                    if n >= 2:
                        dve.wait_ge(level_ready, of(c, NL + 1, n))
                    else:
                        wait(dve, level_ready, of(c, NL + 1, 0))
                    ev, zv = level(ebuf[:, n % 2, :], b), level(zbuf[:, n % 2, :], b)
                    nc.vector.tensor_tensor(zv[:, :, 1, :], ev[:, :, 1, :], level(q_all, b)[:, :, 1, :], ALU.mult)
                    nc.vector.tensor_tensor(zv[:, :, 0, :], ev[:, :, 0, :], level(k_all, b)[:, :, 0, :],
                                            ALU.mult).then_inc(z_done, 1)
                    keep(n)
                    if n == 2 and not first:
                        turn_lo(c - 1)
                    if n == 3 and not last:
                        log_sigmoid(c + 1)
                    if n == 4:
                        dve.wait_ge(q_exp, c + 1)
                        nc.vector.tensor_tensor(q_dec[:, :, :], q_dec[:, :, :], qk[:, 0:H, :], ALU.mult
                                                ).then_inc(qk_decayed, 1)
                    if n == 5 and not last:
                        dve.wait_ge(k_exp, of(c, H, H))
                        nc.vector.tensor_tensor(k_dec[:, :, :], k_dec[:, :, :], qk[:, H:2 * H, :], ALU.mult
                                                ).then_inc(qk_decayed, 1)
                keep(NL)
                if not last:
                    scale_q(c + 1)
                    dve.wait_ge(last_exp, c + 1)
                    for h in range(H):
                        dve.wait_ge(s_ready, of(c, 2, h // 2 + 1))
                        nc.vector.scalar_tensor_tensor(
                            out=state[:, h, :], in0=state[:, h, :], scalar=eb_last[:, h:h + 1],
                            in1=ps[:, 3 - h // 2, (h % 2) * DV:(h % 2 + 1) * DV], op0=ALU.mult, op1=ALU.add
                        ).then_inc(state_done, 1)
                dve.wait_ge(o_root, c + 1)
                nc.vector.reciprocal(ostat[:, 2, :], ostat[:, 1, :]).then_inc(o_inv, 1)
                dve.wait_ge(o_inv, c + 1)
                dve.wait_ge(g_gained, c + 1)
                for h in range(H):
                    y = nc.vector.scalar_tensor_tensor(
                        out=g_sb[:, h * DV:(h + 1) * DV], in0=ps[:, 6 + h // 2, (h % 2) * DV:(h % 2 + 1) * DV],
                        scalar=ostat[:, 2, h:h + 1], in1=g_sb[:, h * DV:(h + 1) * DV], op0=ALU.mult, op1=ALU.mult)
                y.then_inc(y_done, 1)

            loop(dve, NC, chunk)
            for q in range(2 * TT):
                t, ch = q % TT, q // TT
                dve.wait_ge(ao_ready, q + 1)
                if q == 0:
                    dve.wait_ge(xr_ld[0], 16 * 3)
                if q == 3:
                    dve.wait_ge(xr_ld[1], 16 * (TT - 3))
                nc.vector.tensor_tensor(resid[:, t, half(ch)], resid[:, t, half(ch)], ps[:, 4 + q % 4, :], ALU.add
                                        ).then_inc(ao_added, 1)
                if q == 0:
                    turn_lo(NC - 1)
                if ch and t >= 1:
                    norm_apply(dve, 1, t - 1, resid[:, t - 1, :], work[:, (t - 1) % 2, :])
                if ch and t >= 2:
                    norm_lo(dve, 1, t - 2)
            norm_apply(dve, 1, TT - 1, resid[:, TT - 1, :], work[:, (TT - 1) % 2, :])
            norm_lo(dve, 1, TT - 2)
            norm_lo(dve, 1, TT - 1)

            def add_down(i, ready, added, n, turned_too, behind=None):
                def normalised(t):
                    return work[:, t % 2, :] if turned_too else out_slot(t)

                for t in range(TT):
                    for ch in range(2):
                        q = 2 * t + ch
                        dve.wait_ge(ready, of(i, 16, q + 1))
                        nc.vector.tensor_tensor(resid[:, t, half(ch)], resid[:, t, half(ch)], ps[:, 4 + q % 4, :],
                                                ALU.add).then_inc(added, 1)
                    if behind is not None and t >= 4:
                        behind(t)
                    if n is not None:
                        if t >= 1:
                            norm_apply(dve, n, t - 1, resid[:, t - 1, :], normalised(t - 1))
                        if t >= 2 and turned_too:
                            norm_lo(dve, n, t - 2)
                if n is not None:
                    norm_apply(dve, n, TT - 1, resid[:, TT - 1, :], normalised(TT - 1))
                    if turned_too:
                        norm_lo(dve, n, TT - 2)
                        norm_lo(dve, n, TT - 1)

            def ffn_dve(layer, n):
                s = fsem[layer]

                def step(i, last):
                    for p in range(4):
                        hf, j = p // 2, p % 2
                        dve.wait_ge(s["silu_done"], of(i, 4, p + 1))
                        dve.wait_ge(s["up_ready"], of(i, 4, p + 1))
                        wait(dve, s["h_hi_done"], of(i, 4, p - 1))
                        nc.vector.tensor_tensor(prod[:, p % 2, :], work[:, 0, half(p % 2)], ps[:, 2 + p % 2, :],
                                                ALU.mult).then_inc(s["prod_done"], 1)
                        dve.wait_ge(s["h_hi_done"], of(i, 4, p + 1))
                        nc.vector.tensor_tensor(h_lo[:, j, half(hf)], prod[:, p % 2, :],
                                                f32(h_hi[:, j, half(hf)]), ALU.subtract).then_inc(s["h_lo_done"], 1)
                    add_down(i, s["down_ready"], s["down_added"], n if last else None, n != 4)
                loop(dve, FSTEPS, step)

            ffn_dve(0, 2)

            def gv(i, last):
                def stat(par, t):
                    dve.wait_ge(gv_gelu, of(i, 16, 8 * par + t + 1))
                    nc.vector.bn_stats(st6[:, t, :], vg[:, t % 4, :]).then_inc(gv_stat, 1)

                for par in range(2):
                    dve.wait_ge(bias_ld[par], of(i, 16, 16))
                    for t in range(TT):
                        dve.wait_ge(gv_ready, of(i, 16, 8 * par + t + 1))
                        wait(dve, gv_gelu, of(i, 16, 8 * par + t - 1))
                        nc.vector.tensor_tensor(vb[:, t % 2, :], ps[:, 4 + t % 4, :], v_bias[:, par, :], ALU.add
                                                ).then_inc(gv_biased, 1)
                        if t == 0:
                            wait(dve, gv_kept, of(i, 2, par))
                        if t >= 1:
                            stat(par, t - 1)
                    stat(par, TT - 1)
                    dve.wait_ge(gv_stat, of(i, 16, 8 * par + 8))
                    nc.vector.tensor_scalar(st_all[:, :, bass.ds(i * 2 + par, 1), :],
                                            st6[:, :, :].rearrange("p t (g s) -> p t g s", g=1), 1.0, None, ALU.mult
                                            ).then_inc(gv_kept, 1)

            loop(dve, VP // 2, gv)
            dve.wait_ge(gv_kept, VP)
            for t in range(TT):
                nc.vector.bn_aggr(mv[:, t, :], st_all[:, t, :, :].rearrange("p g s -> p (g s)")).then_inc(mv_done, 1)
            dve.wait_ge(dev_done, 1)
            nc.vector.reciprocal(dev[:, :], dev[:, :]).then_inc(inv_done, 1)
            dve.wait_ge(inv_done, 1)

            def layer_norm(g, t0, n):
                dve.wait_ge(ln_ld, of(g, 32, 32))
                dve.wait_ge(vn_ld[t0 // 4], of(g, 64, 64))
                for t in range(t0, t0 + n):
                    nc.vector.scalar_tensor_tensor(out=vn[:, t, :], in0=vn[:, t, :], scalar=mv[:, t, 0:1],
                                                   in1=ln_g_bc[:, :], op0=ALU.subtract, op1=ALU.mult
                                                   ).then_inc(vn_centred, 1)
                for t in range(t0, t0 + n):
                    dve.wait_ge(vn_centred, of(g, TT, t + 1))
                    nc.vector.scalar_tensor_tensor(out=vn[:, t, :], in0=vn[:, t, :], scalar=dev[:, t:t + 1],
                                                   in1=ln_b_bc[:, :], op0=ALU.mult, op1=ALU.add
                                                   ).then_inc(vn_done, 1)

            def mask_spatial(g):
                dve.wait_ge(ws_turned, g + 1)
                wait(dve, sv_ready, of(g, 6, 0))
                nc.vector.tensor_tensor(ws_t[:, :], ps[:, 1, 0:P], causal[:, :], ALU.mult).then_inc(ws_masked, 1)

            mask_spatial(0)
            layer_norm(0, 0, 4)
            layer_norm(0, 4, 4)

            def gp(g, last):
                if not isinstance(g, int) or g:
                    mask_spatial(g)
                dve.wait_ge(bu_ld, of(g, 32, 32))
                for q in range(6):
                    hf, e = q // 3, q % 3
                    t1 = work[:, 1, half(q % 2)]
                    dve.wait_ge(sv_ready, of(g, 6, q + 1))
                    wait(dve, m_hi_done, of(g, 6, q - 1))
                    nc.vector.tensor_tensor(k4(t1), k4(ps[:, 2 + q % 2, :]),
                                            bs_bc[:, :].rearrange("p (o t) -> p o t", o=1).to_broadcast([P, 4, P]),
                                            ALU.add).then_inc(sv_biased, 1)
                    dve.wait_ge(sv_biased, of(g, 6, q + 1))
                    dve.wait_ge(gu_gelu, of(g, 6, q + 1))
                    nc.vector.tensor_tensor(t1, t1, work[:, 0, half(q % 2)], ALU.mult).then_inc(m_done, 1)
                    dve.wait_ge(m_hi_done, of(g, 6, q + 1))
                    nc.vector.tensor_tensor(m_lo[:, e, half(hf)], t1, f32(m_hi[:, e, half(hf)]), ALU.subtract
                                            ).then_inc(m_lo_done, 1)

                def norm_two(t):
                    layer_norm(g + 1, 2 * (t - 4), 2)

                add_down(g, go_ready, go_added, 3 if last else None, True, None if last else norm_two)

            loop(dve, G, gp)
            ffn_dve(1, 4)

        @block.tensor
        def _(pe):
            pe.wait_ge(ident_ld, 16)
            for t in range(TT // 2):
                norm_turn(pe, 0, t, xn0[:, t % 2, :])
            pe.wait_ge(x_lo_done[0], TT)

            def gate_logits(c):
                pe.wait_ge(al_ld, of(c, 16, 16))
                if not isinstance(c, int) or c > 0:
                    pe.wait_ge(state_done, of(c, H, 2 - H))
                pe.matmul(ps[:, 2, :], al_c[:, :], w_gate2[:, :], start=True, stop=True).then_inc(z_ready, 1)

            def cumulate(c):
                pe.wait_ge(log_a_done, c + 1)
                for h in range(H):
                    mm = pe.matmul(ps[:, 3, tile(h)], log_a[:, tile(h)], causal[:, :], start=True, stop=True)
                mm.then_inc(cum_ready, 1)

            for m in range(4):
                if m == 1:
                    pe.wait_ge(wa_lo_done, 1)
                    for h in range(HALVES):
                        for k in range(KT):
                            for part in (x_hi, x_lo):
                                mm = pe.matmul(ps[0:2 * RANK, 2 * h, :], wa_parts[:, k, :], part[:, k, half(h)],
                                               start=(k == 0 and part is x_hi), stop=(k == KT - 1 and part is x_lo))
                        mm.then_inc(al_ready, 1)
                for j in range(8):
                    q = 8 * m + j
                    if q == 4:
                        pe.wait_ge(x_lo_done[0], 2 * TT)
                    if q == 28:
                        pe.wait_ge(const_ld, 16 * 6)
                        pe.wait_ge(ones_ld, 16)
                        gate_logits(0)
                    if q == 31:
                        cumulate(0)
                    if j < 4 and m:
                        wait(pe, qk_copied if m % 2 else v_copied, 8 * ((m - 1) // 2) + j + 5)
                    elif j >= 4:
                        wait(pe, v_copied if m % 2 else qk_copied, 8 * (m // 2) + j - 3)
                    for k in range(KT):
                        if j == 0:
                            block_cut(pe, "gla", 0, 8 * m + k)
                        at = at_gla(m, k)
                        if m % 2 == 0:
                            col = at + (j % H) * P
                            mm = product(pe, ps[:, 4 + q % 4, :], w_hi(col, P), w_lo(col, P),
                                         x_hi[:, k, half(j // H)], x_lo[:, k, half(j // H)], k, k == KT - 1)
                        else:
                            mm = product(pe, ps[:, 4 + q % 4, :], x_hi[:, k, tile(j)], x_lo[:, k, tile(j)],
                                         w_hi(at, BANK), w_lo(at, BANK), k, k == KT - 1)
                        if q == 3 and k == 3:
                            norm_turn(pe, 0, 7, xn0[:, 1, :])
                    mm.then_inc(proj_ready, 1)
                    if q < 3:
                        norm_turn(pe, 0, 4 + q, xn0[:, q % 2, :])
            pe.wait_ge(state_done, 2)

            def turn_y(c):
                pe.wait_ge(y_done, c + 1)
                for k in range(KT):
                    mm = pe.transpose(ps[:, 6 + k // 4, tile(k % 4)], g_sb[:, tile(k)], ident[:, :])
                    if k % 4 == 3:
                        mm.then_inc(y_turned, 1)

            def chunk(c, last):
                first = isinstance(c, int) and c == 0

                def gate(b, k0, k1):
                    if b == 0:
                        pe.wait_ge(xc_ld, of(c, 32, 32))
                    if k0 == 0:
                        wait(pe, g_silu, of(c, 2, b - 1))
                    for k in range(k0, k1):
                        if first:
                            block_cut(pe, "gla", 0, 8 * (4 + b) + k)
                        at = at_gla(4 + b, k)
                        mm = product(pe, ps[:, b, :], xc_hi[:, k, :], xc_lo[:, k, :], w_hi(at, BANK), w_lo(at, BANK),
                                     k, k == KT - 1)
                    if k1 == KT:
                        mm.then_inc(g_ready, 1)

                def lvl(n):
                    if not first or n >= 2:
                        pe.wait_ge(level_kept, of(c, NL + 1, n - 1))
                    else:
                        pe.wait_ge(v_copied, 13 if n == 0 else 16)
                    if n == 0:
                        pe.wait_ge(q_scaled, c + 1)
                    else:
                        pe.wait_ge(z_done, of(c, NL, n))
                    for h in range(H):
                        z = zbuf[:, (n - 1) % 2, tile(h)]
                        if n == 1:
                            mm = pe.matmul(ps[0:HC, 5, h * CH + HC:(h + 1) * CH], z[:, 0:HC], z[:, HC:CH],
                                           start=True, stop=True)
                            continue
                        mm = pe.matmul(ps[:, 4 + n % 2, tile(h)], qk[:, H + h, :] if n == 0 else z,
                                       qk[:, h, :] if n == 0 else z, start=True, stop=True)
                    mm.then_inc(level_ready, 1)

                gate(0, 0, KT)
                lvl(0)
                lvl(1)
                if not last:
                    gate_logits(c + 1)
                if not first:
                    turn_y(c - 1)
                lvl(2)
                gate(1, 0, KT // 2)
                lvl(3)
                lvl(4)
                gate(1, KT // 2, 6)
                if not last:
                    cumulate(c + 1)
                lvl(5)
                gate(1, 6, 7)
                lvl(6)
                gate(1, 7, KT)
                lvl(7)
                if not last:
                    pe.wait_ge(qk_decayed, of(c, 2, 2))
                    for h in range(H):
                        mm = pe.transpose(ps[:, 2, tile(h)], k_dec[:, h, :], ident[:, :])
                    mm.then_inc(k_turned, 1)
                if last:
                    pe.wait_ge(qk_decayed, 2 * c + 1)
                wait(pe, y_lo_done, of(c, 2, 0))
                wait(pe, state_done, of(c, H, 2))
                def o(h):
                    return ps[:, 6 + h // 2, (h % 2) * DV:(h % 2 + 1) * DV]

                for h in range(0, H, 2):
                    pe.matmul(o(h), q_dec[:, h, :], state[:, h, :], start=True, stop=False)
                pe.wait_ge(level_kept, of(c, NL + 1, NL + 1))
                pe.wait_ge(v_ld, of(c, 16, 16))
                for h in range(H):
                    if h % 2:
                        pe.matmul(o(h), q_dec[:, h, :], state[:, h, :], start=True, stop=False)
                    mm = pe.matmul(o(h), att[:, h, :], v_sb[:, h * DV:(h + 1) * DV], start=False, stop=True)
                    if h % 2:
                        mm.then_inc(o_ready, 1)
                if not last:
                    pe.wait_ge(k_dec_t_done, c + 1)
                    pe.wait_ge(bcum_done, c + 2)
                    for h in range(H):
                        mm = pe.matmul(ps[:, 3 - h // 2, (h % 2) * DV:(h % 2 + 1) * DV], k_dec_t[:, h, :],
                                       v_sb[:, h * DV:(h + 1) * DV], start=True, stop=True)
                        if h % 2:
                            mm.then_inc(s_ready, 1)

            loop(pe, NC, chunk)
            for q in range(2 * TT):
                t, ch = q % TT, q // TT
                wait(pe, ao_added, q - 3)
                if ch == 0:
                    pe.wait_ge(y_moved, 32 * (t + 1))
                if q == 2:
                    pe.wait_ge(y_lo_done, 2 * NC)
                for k in range(KT):
                    if t == 0:
                        block_cut(pe, "gla", 0, 48 + 8 * ch + k)
                    at = at_gla(6 + ch, k)
                    mm = product(pe, ps[:, 4 + q % 4, :], x_hi[:, k, tile(t)], x_lo[:, k, tile(t)], w_hi(at, BANK),
                                 w_lo(at, BANK), k, k == KT - 1)
                    if q == 1 and k == 3:
                        turn_y(NC - 1)
                mm.then_inc(ao_ready, 1)
                if ch and t >= 2:
                    norm_turn(pe, 1, t - 2, work[:, (t - 2) % 2, :])

            def ffn_pe(layer, n_in, n):
                s, name = fsem[layer], f"ffn{layer}"

                def step(i, last):
                    first = isinstance(i, int) and i == 0
                    for p in range(4):
                        hf, j = p // 2, p % 2
                        if first:
                            pe.wait_ge(x_lo_done[n_in], TT + 2 if p == 0 else 2 * TT)
                        wait(pe, s["silu_done"], of(i, 4, p - 1))
                        for which, bank in ((0, p % 2), (1, 2 + p % 2)):
                            if which:
                                wait(pe, s["prod_done"], of(i, 4, p - 1))
                            for k in range(KT):
                                if p == 0 and which == 0:
                                    block_cut(pe, name, i, k)
                                col = at_ffn(k) + which * FC + j * P
                                mm = product(pe, ps[:, bank, :], w_hi(col, P), w_lo(col, P), x_hi[:, k, half(hf)],
                                             x_lo[:, k, half(hf)], k, k == KT - 1)
                                if first and p == 0 and which == 0 and k == 3:
                                    norm_turn(pe, n_in, TT - 2, work[:, (TT - 2) % 2, :])
                            mm.then_inc(s["up_ready" if which else "gate_ready"], 1)
                            if first and p == 0 and which == 0:
                                norm_turn(pe, n_in, TT - 1, work[:, (TT - 1) % 2, :])
                    for t in range(TT):
                        if t % 4 == 0:
                            pe.wait_ge(s["h_lo_done"], of(i, 4, 2 + t // 2))
                        for ch in range(2):
                            q = 2 * t + ch
                            wait(pe, s["down_added"], of(i, 16, q - 3))
                            for k in range(FT):
                                if q == 0 or (q == 1):
                                    block_cut(pe, name, i, 8 + 2 * k + ch)
                                at = at_ffn(8 + 2 * k + ch)
                                mm = product(pe, ps[:, 4 + q % 4, :], h_hi[:, k, tile(t)], h_lo[:, k, tile(t)],
                                             w_hi(at, BANK), w_lo(at, BANK), k, k == FT - 1)
                            mm.then_inc(s["down_ready"], 1)
                        if last and n != 4 and t >= 2:
                            norm_turn(pe, n, t - 2, work[:, (t - 2) % 2, :])
                loop(pe, FSTEPS, step)

            ffn_pe(0, 1, 2)

            def gv(i, last):
                first = isinstance(i, int) and i == 0
                for par in range(2):
                    for t in range(TT):
                        if first and par == 0:
                            pe.wait_ge(x_lo_done[2], 2 * t + 2)
                        wait(pe, gv_biased, of(i, 16, 8 * par + t - 3))
                        for k in range(KT):
                            if t == 0:
                                block_cut(pe, "gv", i, 8 * par + k)
                            at = at_gv(8 * par + k)
                            mm = product(pe, ps[:, 4 + t % 4, :], x_hi[:, k, tile(t)], x_lo[:, k, tile(t)],
                                         w_hi(at, BANK, h_hi_flat), w_lo(at, BANK, h_lo_flat), k, k == KT - 1)
                        mm.then_inc(gv_ready, 1)
                        if first and par == 0 and t < 2:
                            norm_turn(pe, 2, TT - 2 + t, work[:, (TT - 2 + t) % 2, :])

            loop(pe, VP // 2, gv)

            def gp(g, last):
                pe.wait_ge(ws_ld, of(g, 16, 16))
                wait(pe, gu_gelu, of(g, 6, 0))
                pe.transpose(ps[:, 1, 0:P], ws_raw[:, :], ident[:, :]).then_inc(ws_turned, 1)

                def spatial(q):
                    hf, e = q // 3, q % 3
                    if q == 0:
                        pe.wait_ge(ws_masked, g + 1)
                    pe.wait_ge(vn_done, of(g, TT, 4 * hf + 4))
                    wait(pe, sv_biased, of(g, 6, q - 1))
                    for c in range(4):
                        mm = pe.matmul(ps[:, 2 + q % 2, tile(c)], vn[:, 4 * hf + c, tile(e)], ws_t[:, :],
                                       start=True, stop=True)
                    mm.then_inc(sv_ready, 1)

                for q in range(6):
                    hf, e = q // 3, q % 3
                    wait(pe, gu_gelu, of(g, 6, q - 1))
                    if q == 1:
                        pe.wait_ge(ws_masked, g + 1)
                    for k in range(KT):
                        if q == 0:
                            block_cut(pe, "gp", g, k)
                        col = at_gp(k) + e * P
                        mm = product(pe, ps[:, q % 2, :], w_hi(col, P), w_lo(col, P), x_hi[:, k, half(hf)],
                                     x_lo[:, k, half(hf)], k, k == KT - 1)
                    mm.then_inc(gu_ready, 1)
                    if q >= 1:
                        spatial(q - 1)
                spatial(5)
                for t in range(TT):
                    if t % 4 == 0:
                        pe.wait_ge(m_lo_done, of(g, 6, 3 + 3 * (t // 4)))
                    for ch in range(2):
                        q = 2 * t + ch
                        wait(pe, go_added, of(g, 16, q - 3))
                        for k in range(GE):
                            if t == 0:
                                block_cut(pe, "gp", g, 8 + 2 * k + ch)
                            at = at_gp(8 + 2 * k + ch)
                            mm = product(pe, ps[:, 4 + q % 4, :], m_hi[:, k, tile(t)], m_lo[:, k, tile(t)],
                                         w_hi(at, BANK), w_lo(at, BANK), k, k == GE - 1)
                        mm.then_inc(go_ready, 1)
                    if last and t >= 2:
                        norm_turn(pe, 3, t - 2, work[:, (t - 2) % 2, :])

            loop(pe, G, gp)
            ffn_pe(1, 3, 4)


_INS = ["x", "norm_mix", "norm_ffn", "norm_final", "w_ffn_gate", "w_ffn_up", "w_ffn_down",
        "a_w_in", "a_w_gate2", "a_b_gate", "a_g_norm", "a_w_out",
        "b_w_in", "b_b_in", "b_ln_g", "b_ln_b", "b_w_s", "b_b_s", "b_w_out"]


def _constants():
    s, t = np.arange(P)[:, None], np.arange(P)[None, :]
    levels = [s == t] + [(s // (2 * b) == t // (2 * b)) & (s // b % 2 == 0) & (t // b % 2 == 1) for b in LEVELS]
    return {"level_masks": np.stack(levels, 1).astype(np.float32),
            "causal_matrix": (s <= t).astype(np.float32),
            "identity": np.eye(P, dtype=np.float32)}


def kernel(**inputs):
    import concourse.bacc as bacc
    from concourse.bass_utils import run_bass_kernel_spmd

    nc = bacc.Bacc("TRN2", target_bir_lowering=False, num_devices=1)
    arrays, args = {}, []
    given = {n: np.ascontiguousarray(inputs[n]) for n in _INS}
    given.update(_constants())
    for name, a in given.items():
        arrays[f"in_{name}"] = a
        args.append(nc.dram_tensor(f"in_{name}", a.shape, mybir.dt.from_np(a.dtype), kind="ExternalInput").ap())
    shape = given["x"].shape
    args.append(nc.dram_tensor("out_0", shape, F32, kind="ExternalOutput").ap())
    trunk_kernel(nc, *args)
    r = run_bass_kernel_spmd(nc, [arrays], core_ids=[0])
    return r.results[0]["out_0"]
```
